# Optimizing a Trainium2 kernel written in Bass

```python
import math
import jax, jax.numpy as jnp
from jax import lax
import numpy as np

D_MODEL = 1024
BATCH = 1
SEQ = 1024
DEPTH = 1
DEC_BATCH = 8
DEC_SEQ = 4
PAST_LEN = 1024
PAGE_SIZE = 128

A_HEADS = 8
A_HD = 64
A_QK = 2 * A_HD
A_DV = 2 * A_HD
ROPE_THETA = 10000.0
Q_BLOCK = 128
B_HEADS = 8
B_DK = 128
B_DV = 128
CONV_W = 4
DN_CHUNK = 64
D_FF = 2816
NORM_EPS = 1e-6

A_Q_WIDTH = A_HEADS * A_QK
A_V_WIDTH = A_HEADS * A_DV
B_K_WIDTH = B_HEADS * B_DK
B_V_WIDTH = B_HEADS * B_DV
CONV_CH = 2 * B_K_WIDTH + B_V_WIDTH
IN_SPLITS = (A_Q_WIDTH, A_Q_WIDTH, A_V_WIDTH, CONV_CH, B_V_WIDTH, B_HEADS, B_HEADS, D_MODEL, D_MODEL)
D_IN = sum(IN_SPLITS)

kernel_name = "hybrid_diffattn_gdn_macaron_step"

def rmsnorm(x, w):
    xf = x.astype(jnp.float32)
    y = xf * lax.rsqrt(jnp.mean(xf * xf, axis=-1, keepdims=True) + NORM_EPS) * w.astype(jnp.float32)
    return y.astype(x.dtype)

def l2norm(x):
    xf = x.astype(jnp.float32)
    return xf * lax.rsqrt(jnp.sum(xf * xf, axis=-1, keepdims=True) + NORM_EPS)

def swiglu(x, w_in, w_out):
    gate, up = jnp.split(x @ w_in, 2, axis=-1)
    return (jax.nn.silu(gate) * up) @ w_out

def rope(x, pos):
    d = x.shape[-1]
    half = d // 2
    inv = jnp.power(ROPE_THETA, -2.0 * jnp.arange(half, dtype=jnp.float32) / d)
    ang = pos.astype(jnp.float32)[:, None] * inv[None, :]
    bshape = (pos.shape[0],) + (1,) * (x.ndim - 3) + (half,)
    cos = jnp.cos(ang).reshape(bshape)
    sin = jnp.sin(ang).reshape(bshape)
    xf = x.astype(jnp.float32)
    x1, x2 = xf[..., :half], xf[..., half:]
    return jnp.concatenate([x1 * cos - x2 * sin, x2 * cos + x1 * sin], axis=-1).astype(x.dtype)

def diff_attn_block(q, k, v, q_pos, k_pos, lam):
    s = jnp.einsum('bqhmd,bkhmd->mbhqk', q, k)
    mask = k_pos[None, :] <= q_pos[:, None]
    p = jax.nn.softmax(jnp.where(mask, s, -jnp.inf), axis=-1)
    return jnp.einsum('bhqk,bkhd->bqhd', p[0] - lam * p[1], v)

def diff_attention(q, k, v, q_pos, past_k, past_v, lam):
    B, L = q.shape[:2]
    k_rows = k.reshape(B, L, A_HEADS, A_QK)
    if past_k is None:
        k_all, v_all, k_pos = k_rows, v, q_pos
    else:
        k_all = jnp.concatenate([past_k.astype(k_rows.dtype), k_rows], axis=1)
        v_all = jnp.concatenate([past_v.astype(v.dtype), v], axis=1)
        k_pos = jnp.arange(k_all.shape[1], dtype=jnp.int32)
    kf = k_all.astype(jnp.float32).reshape(B, k_all.shape[1], A_HEADS, 2, A_HD)
    vf = v_all.astype(jnp.float32)
    qf = q.astype(jnp.float32) * (A_HD ** -0.5)
    if L > Q_BLOCK and L % Q_BLOCK == 0:
        nb = L // Q_BLOCK
        qb = jnp.moveaxis(qf.reshape(B, nb, Q_BLOCK, A_HEADS, 2, A_HD), 1, 0)
        pb = q_pos.reshape(nb, Q_BLOCK)
        o = lax.map(lambda t: diff_attn_block(t[0], kf, vf, t[1], k_pos, lam), (qb, pb))
        o = jnp.moveaxis(o, 0, 1).reshape(B, L, A_HEADS, A_DV)
    else:
        o = diff_attn_block(qf, kf, vf, q_pos, k_pos, lam)
    return o, k_rows

def gated_delta_chunked(q, k, v, g, beta, S0):
    B, H, L, dk = q.shape
    dv = v.shape[-1]
    C = DN_CHUNK
    pad = (-L) % C
    if pad:
        pw = ((0, 0), (0, 0), (0, pad))
        q = jnp.pad(q, pw + ((0, 0),))
        k = jnp.pad(k, pw + ((0, 0),))
        v = jnp.pad(v, pw + ((0, 0),))
        g = jnp.pad(g, pw)
        beta = jnp.pad(beta, pw)
    n = (L + pad) // C
    q = (q * (dk ** -0.5)).reshape(B, H, n, C, dk)
    k = k.reshape(B, H, n, C, dk)
    v = v.reshape(B, H, n, C, dv)
    gc = jnp.cumsum(g.reshape(B, H, n, C), axis=-1)
    beta = beta.reshape(B, H, n, C)
    idx = jnp.arange(C)
    incl = idx[:, None] >= idx[None, :]
    strict = idx[:, None] > idx[None, :]
    decay = jnp.exp(jnp.where(incl, gc[..., :, None] - gc[..., None, :], -jnp.inf))
    kb = k * beta[..., None]
    lower = jnp.where(strict, jnp.einsum('bhncd,bhnmd->bhncm', kb, k) * decay, 0.0)
    rhs = jnp.concatenate([v * beta[..., None], kb * jnp.exp(gc)[..., None]], axis=-1)
    sol = lax.linalg.triangular_solve(jnp.eye(C, dtype=q.dtype) + lower, rhs, left_side=True, lower=True)
    u, w = sol[..., :dv], sol[..., dv:]
    qk = jnp.einsum('bhncd,bhnmd->bhncm', q, k) * decay
    q_dec = q * jnp.exp(gc)[..., None]
    k_dec = k * jnp.exp(gc[..., -1:] - gc)[..., None]
    g_tot = jnp.exp(gc[..., -1])
    xs = tuple(jnp.moveaxis(t, 2, 0) for t in (u, w, qk, q_dec, k_dec, g_tot))

    def step(S, inp):
        u_i, w_i, qk_i, qd_i, kd_i, gt_i = inp
        v_new = u_i - jnp.einsum('bhcd,bhde->bhce', w_i, S)
        o_i = jnp.einsum('bhcd,bhde->bhce', qd_i, S) + jnp.einsum('bhcm,bhme->bhce', qk_i, v_new)
        S = S * gt_i[..., None, None] + jnp.einsum('bhcd,bhce->bhde', kd_i, v_new)
        return S, o_i

    S, o = lax.scan(step, S0, xs)
    o = jnp.moveaxis(o, 0, 2).reshape(B, H, n * C, dv)[:, :, :L]
    return o, S

def gated_deltanet(qkv, z, a, b, conv_state, S0, conv_w, a_log, dt_bias, norm_w):
    B, L = qkv.shape[:2]
    xp = jnp.concatenate([conv_state.astype(qkv.dtype), qkv], axis=1)
    new_conv = xp[:, L:]
    c = xp[:, 0:L] * conv_w[0]
    for i in range(1, CONV_W):
        c = c + xp[:, i:i + L] * conv_w[i]
    c = jax.nn.silu(c)
    q, k, v = jnp.split(c, [B_K_WIDTH, 2 * B_K_WIDTH], axis=-1)
    q = l2norm(q.reshape(B, L, B_HEADS, B_DK))
    k = l2norm(k.reshape(B, L, B_HEADS, B_DK))
    v = v.reshape(B, L, B_HEADS, B_DV).astype(jnp.float32)
    beta = jax.nn.sigmoid(b.astype(jnp.float32))
    g = -jnp.exp(a_log.astype(jnp.float32)) * jax.nn.softplus(a.astype(jnp.float32) + dt_bias.astype(jnp.float32))
    tr = lambda t: jnp.swapaxes(t, 1, 2)
    o, S = gated_delta_chunked(tr(q), tr(k), tr(v), tr(g), tr(beta), S0.astype(jnp.float32))
    o = rmsnorm(tr(o), norm_w) * jax.nn.silu(z.reshape(B, L, B_HEADS, B_DV).astype(jnp.float32))
    return o.reshape(B, L, B_V_WIDTH).astype(qkv.dtype), new_conv, S.astype(S0.dtype)

def decoder_layer(x, pos, past_k, past_v, conv_state, delta_state, p, layer_idx):
    B, L = x.shape[:2]
    h = x + 0.5 * rmsnorm(swiglu(rmsnorm(x, p['ffn1_pre']), p['ffn1_w_in'], p['ffn1_w_out']), p['ffn1_post'])
    u = rmsnorm(h, p['mix_pre'])
    pts = np.cumsum(IN_SPLITS)[:-1].tolist()
    qa, ka, va, qkv_b, z_b, a_b, b_b, gate_a, gate_b = jnp.split(u @ p['w_in'], pts, axis=-1)
    qa = rope(qa.reshape(B, L, A_HEADS, 2, A_HD), pos)
    ka = rope(ka.reshape(B, L, A_HEADS, 2, A_HD), pos)
    va = va.reshape(B, L, A_HEADS, A_DV)
    lam_init = 0.8 - 0.6 * math.exp(-0.3 * layer_idx)
    f32 = jnp.float32
    lam = (jnp.exp(jnp.sum(p['lq1'].astype(f32) * p['lk1'].astype(f32)))
           - jnp.exp(jnp.sum(p['lq2'].astype(f32) * p['lk2'].astype(f32))) + lam_init)
    o_a, k_rows = diff_attention(qa, ka, va, pos, past_k, past_v, lam)
    o_a = (rmsnorm(o_a, p['attn_subln']) * (1.0 - lam_init)).reshape(B, L, A_V_WIDTH).astype(x.dtype)
    branch_a = o_a @ p['w_a_out']
    o_b, new_conv, new_S = gated_deltanet(qkv_b, z_b, a_b, b_b, conv_state, delta_state, p['conv_w'],
                                          p['a_log'], p['dt_bias'], p['delta_norm'])
    branch_b = o_b @ p['w_b_out']
    merged = jax.nn.sigmoid(gate_a) * branch_a + jax.nn.sigmoid(gate_b) * branch_b
    h = h + rmsnorm(merged @ p['w_o'], p['mix_post'])
    y = h + 0.5 * rmsnorm(swiglu(rmsnorm(h, p['ffn2_pre']), p['ffn2_w_in'], p['ffn2_w_out']), p['ffn2_post'])
    return y, k_rows, va, new_conv, new_S

def setup_inputs(seed: int = 0) -> dict:
    key = jax.random.key(seed)
    ks = iter(jax.random.split(key, 40))
    f32 = jnp.float32

    def normal(shape, scale):
        return scale * jax.random.normal(next(ks), shape, f32)

    def gain(shape):
        return 1.0 + normal(shape, 0.05)

    n_pages = PAST_LEN // PAGE_SIZE
    used = DEC_BATCH * n_pages
    n_pool = used + max(1, used // 4)
    page_table = jax.random.permutation(next(ks), n_pool)[:used].reshape(DEC_BATCH, n_pages).astype(jnp.int32)
    dt = jax.random.uniform(next(ks), (DEPTH, B_HEADS), f32, 1e-3, 0.1)
    return {
        'x_prompt': normal((BATCH, SEQ, D_MODEL), 1.0),
        'x_sample': normal((DEC_BATCH, DEC_SEQ, D_MODEL), 1.0),
        'cache_k': normal((DEPTH, n_pool, PAGE_SIZE, A_HEADS, A_QK), 1.0),
        'cache_v': normal((DEPTH, n_pool, PAGE_SIZE, A_HEADS, A_DV), 1.0),
        'state_conv': normal((DEPTH, DEC_BATCH, CONV_W - 1, CONV_CH), 1.0),
        'state_delta': normal((DEPTH, DEC_BATCH, B_HEADS, B_DK, B_DV), 0.1),
        'page_table': page_table,
        'ffn1_pre_norm': gain((DEPTH, D_MODEL)),
        'ffn1_w_in': normal((DEPTH, D_MODEL, 2 * D_FF), D_MODEL ** -0.5),
        'ffn1_w_out': normal((DEPTH, D_FF, D_MODEL), D_FF ** -0.5),
        'ffn1_post_norm': gain((DEPTH, D_MODEL)),
        'mix_pre_norm': gain((DEPTH, D_MODEL)),
        'w_in': normal((DEPTH, D_MODEL, D_IN), D_MODEL ** -0.5),
        'conv_w': normal((DEPTH, CONV_W, CONV_CH), CONV_W ** -0.5),
        'lambda_q1': normal((DEPTH, A_HD), 0.1),
        'lambda_k1': normal((DEPTH, A_HD), 0.1),
        'lambda_q2': normal((DEPTH, A_HD), 0.1),
        'lambda_k2': normal((DEPTH, A_HD), 0.1),
        'attn_subln': gain((DEPTH, A_DV)),
        'a_log': jnp.log(jax.random.uniform(next(ks), (DEPTH, B_HEADS), f32, 1.0, 16.0)),
        'dt_bias': jnp.log(jnp.expm1(dt)),
        'delta_norm': gain((DEPTH, B_DV)),
        'w_a_out': normal((DEPTH, A_V_WIDTH, D_MODEL), A_V_WIDTH ** -0.5),
        'w_b_out': normal((DEPTH, B_V_WIDTH, D_MODEL), B_V_WIDTH ** -0.5),
        'w_o': normal((DEPTH, D_MODEL, D_MODEL), D_MODEL ** -0.5),
        'mix_post_norm': gain((DEPTH, D_MODEL)),
        'ffn2_pre_norm': gain((DEPTH, D_MODEL)),
        'ffn2_w_in': normal((DEPTH, D_MODEL, 2 * D_FF), D_MODEL ** -0.5),
        'ffn2_w_out': normal((DEPTH, D_FF, D_MODEL), D_FF ** -0.5),
        'ffn2_post_norm': gain((DEPTH, D_MODEL)),
    }

def reference(x_prompt, x_sample, cache_k, cache_v, state_conv, state_delta, page_table,
              ffn1_pre_norm, ffn1_w_in, ffn1_w_out, ffn1_post_norm, mix_pre_norm, w_in, conv_w,
              lambda_q1, lambda_k1, lambda_q2, lambda_k2, attn_subln, a_log, dt_bias, delta_norm,
              w_a_out, w_b_out, w_o, mix_post_norm, ffn2_pre_norm, ffn2_w_in, ffn2_w_out, ffn2_post_norm):
    n_pages = PAST_LEN // PAGE_SIZE
    Bp, Lp = x_prompt.shape[:2]
    Bs, Ls = x_sample.shape[:2]
    pos_p = jnp.arange(Lp, dtype=jnp.int32)
    pos_s = PAST_LEN + jnp.arange(Ls, dtype=jnp.int32)
    yp, ys = x_prompt, x_sample
    kp_l, vp_l, cp_l, sp_l, ks_l, vs_l, cs_l, ss_l = [], [], [], [], [], [], [], []
    for i in range(DEPTH):
        p = {
            'ffn1_pre': ffn1_pre_norm[i], 'ffn1_w_in': ffn1_w_in[i], 'ffn1_w_out': ffn1_w_out[i],
            'ffn1_post': ffn1_post_norm[i], 'mix_pre': mix_pre_norm[i], 'w_in': w_in[i], 'conv_w': conv_w[i],
            'lq1': lambda_q1[i], 'lk1': lambda_k1[i], 'lq2': lambda_q2[i], 'lk2': lambda_k2[i],
            'attn_subln': attn_subln[i], 'a_log': a_log[i], 'dt_bias': dt_bias[i], 'delta_norm': delta_norm[i],
            'w_a_out': w_a_out[i], 'w_b_out': w_b_out[i], 'w_o': w_o[i], 'mix_post': mix_post_norm[i],
            'ffn2_pre': ffn2_pre_norm[i], 'ffn2_w_in': ffn2_w_in[i], 'ffn2_w_out': ffn2_w_out[i],
            'ffn2_post': ffn2_post_norm[i],
        }
        zero_conv = jnp.zeros((Bp, CONV_W - 1, CONV_CH), x_prompt.dtype)
        zero_S = jnp.zeros((Bp, B_HEADS, B_DK, B_DV), state_delta.dtype)
        yp, kp, vp, cp, sp = decoder_layer(yp, pos_p, None, None, zero_conv, zero_S, p, i)
        past_k = cache_k[i][page_table].reshape(Bs, n_pages * PAGE_SIZE, A_HEADS, A_QK)
        past_v = cache_v[i][page_table].reshape(Bs, n_pages * PAGE_SIZE, A_HEADS, A_DV)
        ys, ks_, vs_, cs_, ss_ = decoder_layer(ys, pos_s, past_k, past_v, state_conv[i], state_delta[i], p, i)
        kp_l.append(kp); vp_l.append(vp); cp_l.append(cp); sp_l.append(sp)
        ks_l.append(ks_); vs_l.append(vs_); cs_l.append(cs_); ss_l.append(ss_)
    return (yp, ys, jnp.stack(kp_l), jnp.stack(vp_l), jnp.stack(cp_l), jnp.stack(sp_l),
            jnp.stack(ks_l), jnp.stack(vs_l), jnp.stack(cs_l), jnp.stack(ss_l))


_drawn_inputs = setup_inputs


def setup_inputs(seed=0):
    import zlib

    import numpy as np

    out = dict(_drawn_inputs(seed))
    spreads = {}
    factors = {'lambda_k2': 3.655, 'ffn2_post_norm': 3.679}
    for name, (base, spread) in spreads.items():
        noise = np.random.default_rng([zlib.crc32(name.encode()), seed]).standard_normal(out[name].shape)
        drawn = base * np.exp(spread * noise) if base else spread * noise
        out[name] = __import__('jax').numpy.asarray(drawn.astype(out[name].dtype))
    for name, factor in factors.items():
        out[name] = (out[name] * factor).astype(out[name].dtype)
    return out
```

```python
from contextlib import ExitStack

import numpy as np

import concourse.bass as bass
from concourse import mybir

ALU = mybir.AluOpType
ACT = mybir.ActivationFunctionType
F32 = mybir.dt.float32
F32R = mybir.dt.float32r
I32 = mybir.dt.int32
AX = mybir.AxisListType

P = 128
D = 1024
KT = D // P
LP = 1024
NB, LS = 8, 4
NS = NB * LS
T = LP + NS
TT = LP // P
CH = T // 3
FF = 2816
FT = FF // P
BLK = FT // 2
H = 8
HD = 64
PAST = 1024
PG = 128
NPAGE = PAST // PG
EPS = 1e-6
CW = 4
CONV_CH = 3 * H * P
D_IN = 9232
OFF_QKVB, OFF_Z, OFF_AB, OFF_GATE = 3072, 6144, 7168, 7184
LAM_INIT = 0.2
NEG = -1e30
LEVELS = 7

C_ID = 0
C_TRI = C_ID + P
C_CAUS = C_TRI + P
C_LEV = C_CAUS + P
C_ONE = C_LEV + LEVELS * P
C_MEAN = C_ONE + P
C_TRI4 = C_MEAN + P
C_SEQ = C_TRI4 + NS
C_POS = C_SEQ + NB
C_MINUS = C_POS + 16
C_MNEW = C_MINUS + 16
C_SAME = C_MNEW + NB * NS
C_EPS = C_SAME + NS
C_COS = C_EPS + 4
NCONST = C_COS
NROPE = 2 * T


def shape_constants():
    c = np.zeros((P, NCONST), np.float32)
    i = np.arange(P)
    c[:, C_ID:C_ID + P] = np.eye(P)
    c[:, C_TRI:C_TRI + P] = i[:, None] <= i[None, :]
    c[:, C_CAUS:C_CAUS + P] = np.where(i[None, :] <= i[:, None], 0.0, NEG)
    for n in range(LEVELS):
        s = 1 << n
        same = i[:, None] // (2 * s) == i[None, :] // (2 * s)
        c[:, C_LEV + n * P:C_LEV + (n + 1) * P] = same & (i[:, None] // s % 2 == 1) & (i[None, :] // s % 2 == 0)
    c[:, C_ONE:C_ONE + P] = 1.0
    c[:, C_MEAN:C_MEAN + P] = 1.0 / D
    s = np.arange(NS)
    c[:NS, C_TRI4:C_TRI4 + NS] = (s[:, None] // LS == s[None, :] // LS) & (s[:, None] <= s[None, :])
    c[:NS, C_SEQ:C_SEQ + NB] = s[:, None] // LS == np.arange(NB)[None, :]
    c[:NS, C_SAME:C_SAME + NS] = s[:, None] // LS == s[None, :] // LS
    for j in range(4):
        for q in range(LS):
            c[32 * j + q, C_POS + 4 * j + q] = 1.0
            c[32 * j + LS + q, C_MINUS + 4 * j + q] = 1.0
            for m in range(2):
                seen = (s[None, :] // LS == np.arange(NB)[:, None]) & (s[None, :] % LS <= q)
                c[32 * j + LS * m + q, C_MNEW:C_MNEW + NB * NS] = np.where(seen, 0.0, NEG).ravel()
    c[:, C_EPS] = EPS
    c[:, C_EPS + 1] = 4.0 * EPS
    half = HD // 2
    inv = np.power(np.float32(10000.0), np.float32(-2.0) * np.arange(half, dtype=np.float32) / np.float32(HD))
    pos = np.concatenate([np.arange(LP), np.tile(PAST + np.arange(LS), NB)]).astype(np.float32)
    ang = (pos[:, None] * inv[None, :].astype(np.float32)).astype(np.float32)
    cos, sin = np.cos(ang).T, np.sin(ang).T
    r = np.zeros((P, NROPE), np.float32)
    for g in range(4):
        r[32 * g:32 * g + 32, :T] = cos
        r[32 * g:32 * g + 32, T:] = sin if g % 2 else -sin
    return c, r


def cols(c):
    return slice(c * CH, (c + 1) * CH)


def wait(eng, s, value):
    if not (isinstance(value, int) and value <= 0):
        eng.wait_ge(s, value)


def semaphores(nc, ctx, prefix):
    made = []

    def make(name):
        made.append(nc.alloc_semaphore(name=prefix + name))
        return made[-1]

    def give_back():
        nc.clear_and_free_semaphores(made)
        nc.all_engine_barrier()

    ctx.callback(give_back)
    return make


def load_tokens(nc, m, x_prompt, x_sample):
    with ExitStack() as ctx:
        sem = semaphores(nc, ctx, "")
        const_in, turned, moved = sem("ld_const_in"), sem("ld_turned"), sem("ld_moved")
        row_in = [sem("ld_row_in0"), sem("ld_row_in1")]
        rows = ctx.enter_context(nc.sbuf_tensor("rows", [P, 2, D], F32))
        block = ctx.enter_context(nc.Block())
        ident = m.cst[:, C_ID:C_ID + P]
        xp = x_prompt.rearrange("o (t p) d -> (o t) p d", p=P)

        @block.sync
        def _(sp):
            sp.dma_start(m.cst[:, :], m.d_const).then_inc(const_in, 16)
            for k in range(2):
                sp.dma_start(rows[:, k, :], xp[k]).then_inc(row_in[k], 16)
            with sp.Fori(1, TT // 2) as i:
                for k in range(2):
                    sp.wait_ge(turned, 2 * i + k - 1)
                    sp.dma_start(rows[:, k, :], xp[bass.ds(2 * i + k, 1)].rearrange("o p d -> (o p) d")).then_inc(row_in[k], 16)
            sp.wait_ge(turned, TT - 1)
            sp.dma_start(rows[0:NS, 0, :], x_sample.rearrange("b l d -> (b l) d")).then_inc(row_in[0], 16)

        @block.tensor
        def _(pe):
            pe.wait_ge(const_in, 16)

            def turn(k, n):
                for f in range(KT):
                    mm = nc.tensor.transpose(m.ps[:, 2 * k + f // 4, (f % 4) * P:(f % 4) * P + n],
                                             rows[0:n, k, f * P:(f + 1) * P], ident[0:n, 0:n])
                mm.then_inc(turned, 1)

            with pe.Fori(0, TT // 2) as i:
                for k in range(2):
                    pe.wait_ge(row_in[k], 16 * i + 16)
                    pe.wait_ge(moved, 2 * i + k)
                    turn(k, P)
            pe.wait_ge(row_in[0], 16 * (TT // 2) + 16)
            pe.wait_ge(moved, TT)
            turn(0, NS)

        @block.vector
        def _(dve):
            nc.vector.memset(m.scratch[:, :], 0.0).then_inc(moved, 1)
            with dve.Fori(0, TT // 2) as i:
                for k in range(2):
                    dve.wait_ge(turned, 2 * i + k + 1)
                    nc.vector.tensor_copy(m.resid[:, :, bass.ds((2 * i + k) * P, P)],
                                          m.ps[:, 2 * k:2 * k + 2, :].rearrange("p b (f t) -> p (b f) t", t=P)).then_inc(moved, 1)
            dve.wait_ge(turned, TT + 1)
            nc.vector.tensor_copy(m.resid[:, :, LP:T],
                                  m.ps[:, 0:2, :].rearrange("p b (f t) -> p (b f) t", t=P)[:, :, 0:NS]).then_inc(moved, 1)


def small_params(nc, m, gains, subln, dnorm, lams, a_log, dt_bias, state_conv, conv_w):
    with ExitStack() as ctx:
        sem = semaphores(nc, ctx, "")
        par_in, turned, copied, lam_s, lam_e, lam_f, alog_exp = (
            sem("sp_" + n) for n in ("par_in", "turned", "copied", "lam_s", "lam_e", "lam_f", "alog_exp"))
        NG = 6 * KT + 2
        grow = ctx.enter_context(nc.sbuf_tensor("grow", [P, P], F32))
        lrow = ctx.enter_context(nc.sbuf_tensor("lrow", [1, 8, HD], F32))
        crow = ctx.enter_context(nc.sbuf_tensor("crow", [P, CONV_CH], F32))
        block = ctx.enter_context(nc.Block())
        NR = NB * (CW - 1)
        ident = m.cst[:, C_ID:C_ID + P]
        CT = CONV_CH // P

        @block.sync
        def _(sp):
            for n, g in enumerate(gains):
                sp.dma_start(grow[n * KT:(n + 1) * KT, :], g.rearrange("o (f p) -> (o f) p", p=P)).then_inc(par_in, 16)
            sp.dma_start(grow[6 * KT:6 * KT + 1, :], subln).then_inc(par_in, 16)
            sp.dma_start(grow[6 * KT + 1:NG, :], dnorm).then_inc(par_in, 16)
            for n, l in enumerate(lams):
                sp.dma_start(lrow[0:1, n, :], l).then_inc(par_in, 16)
            sp.dma_start(crow[0:NR, :], state_conv.rearrange("o b w c -> (o b w) c")).then_inc(par_in, 16)
            sp.dma_start(crow[NR:NR + CW, :], conv_w.rearrange("o w c -> (o w) c")).then_inc(par_in, 16)
            sp.dma_start(m.alog[0:H, 0:1], a_log.rearrange("o h -> h o")).then_inc(par_in, 16)
            sp.dma_start(m.alog[0:H, 1:2], dt_bias.rearrange("o h -> h o")).then_inc(par_in, 16)

        @block.tensor
        def _(pe):
            pe.wait_ge(par_in, 16 * 16)
            nc.tensor.transpose(m.ps[:, 0, 0:NG], grow[0:NG, :], ident[0:NG, 0:NG]).then_inc(turned, 1)
            for j in range(CT):
                mm = nc.tensor.transpose(m.ps[:, 1 + j // 12, (j % 12) * 32:(j % 12) * 32 + NR + CW],
                                         crow[0:NR + CW, j * P:(j + 1) * P], ident[0:NR + CW, 0:NR + CW])
            mm.then_inc(turned, 1)
            pe.wait_ge(lam_f, 1)
            nc.tensor.matmul(m.ps[:, 3, 0:1], m.cst[0:1, C_ONE:C_ONE + P], lrow[0:1, 7, 2:3],
                             start=True, stop=True).then_inc(turned, 1)

        @block.vector
        def _(dve):
            dve.wait_ge(turned, 1)
            nc.vector.tensor_copy(m.gain[:, :], m.ps[:, 0, 0:NG]).then_inc(copied, 1)
            dve.wait_ge(turned, 2)
            for g in range(2):
                v = m.ps[:, 1 + g, 0:12 * 32].rearrange("p (j r) -> p j r", r=32)
                nc.vector.tensor_copy(m.cst8[:, 12 * g:12 * g + 12, :], v[:, :, 0:NR]).then_inc(copied, 1)
                nc.vector.tensor_copy(m.convw[:, 12 * g:12 * g + 12, :], v[:, :, NR:NR + CW]).then_inc(copied, 1)
            for n in range(2):
                nc.vector.tensor_tensor(lrow[0:1, 4 + n, :], lrow[0:1, 2 * n, :], lrow[0:1, 2 * n + 1, :], ALU.mult).then_inc(lam_s, 1)
            dve.wait_ge(lam_s, 2)
            nc.vector.tensor_reduce(lrow[0:1, 6, 0:2], lrow[0:1, 4:6, :], AX.X, ALU.add).then_inc(lam_s, 1)
            dve.wait_ge(lam_e, 1)
            nc.vector.scalar_tensor_tensor(out=lrow[0:1, 7, 2:3], in0=lrow[0:1, 7, 0:1], scalar=LAM_INIT,
                                           in1=lrow[0:1, 7, 1:2], op0=ALU.add, op1=ALU.subtract).then_inc(lam_f, 1)
            dve.wait_ge(turned, 3)
            nc.vector.tensor_copy(m.lam[:, 0:1], m.ps[:, 3, 0:1]).then_inc(copied, 1)
            dve.wait_ge(copied, 6)
            nc.vector.tensor_scalar(m.lam[:, 1:2], m.lam[:, 0:1], -1.0, None, ALU.mult).then_inc(copied, 1)
            dve.wait_ge(copied, 7)
            nc.vector.scalar_tensor_tensor(out=m.comb[:, :], in0=m.cst[:, C_MINUS:C_MINUS + 16], scalar=m.lam[:, 1:2],
                                           in1=m.cst[:, C_POS:C_POS + 16], op0=ALU.mult, op1=ALU.add).then_inc(copied, 1)

        @block.scalar
        def _(act):
            act.wait_ge(lam_s, 3)
            nc.scalar.activation(lrow[0:1, 7, 0:2], lrow[0:1, 6, 0:2], ACT.Exp).then_inc(lam_e, 1)
            act.wait_ge(par_in, 16 * 16)
            nc.scalar.activation(m.alog[0:H, 2:3], m.alog[0:H, 0:1], ACT.Exp).then_inc(alog_exp, 1)


def norms(nc, m, name, post=None, pre=None):
    HALF = KT // 2
    chunks = ([("post", c) for c in range(3)] if post else []) + ([("pre", c) for c in range(3)] if pre is not None else [])
    with ExitStack() as ctx:
        sem = semaphores(nc, ctx, name)
        squared, summed, logged, rooted, scaled, added, hi_done, lo_pool, lo_dve = (
            sem(n) for n in ("squared", "summed", "logged", "rooted", "scaled", "added", "hi", "lo_pool", "lo_dve"))
        sb = lambda n, s: ctx.enter_context(nc.sbuf_tensor(name + n, s, F32))
        sq = sb("squares", [P, 2, HALF, CH])
        rstd = sb("rstd", [P, 6, CH])
        tmp_pre = sb("tmp_pre", [P, 3, HALF, CH]) if pre is not None else None
        block = ctx.enter_context(nc.Block())

        def tiles(kind, c, a):
            return (post[0] if kind == "post" else m.resid)[:, a * HALF:(a + 1) * HALF, cols(c)]

        by_dve = (2, 5)

        def wait_low(eng, h):
            if h in by_dve:
                eng.wait_ge(lo_dve, 1 + by_dve.index(h))
            else:
                eng.wait_ge(lo_pool, 1 + h - sum(x < h for x in by_dve))

        @block.scalar
        def _(act):
            def squares(k):
                kind, c = chunks[k]
                if kind == "pre" and post:
                    act.wait_ge(added, c + 1)
                for a in range(2):
                    wait(act, summed, 2 * k + a - 1)
                    nc.scalar.activation(sq[:, a, :, :], tiles(kind, c, a), ACT.Square).then_inc(squared, 1)

            def root(k):
                kind, c = chunks[k]
                scale = post[2] ** 2 if kind == "post" else 1.0
                eps = C_EPS + (1 if scale == 4.0 else 0)
                act.wait_ge(summed, 2 * k + 2)
                nc.scalar.activation(rstd[:, k, :], m.ps[:, k, 0:CH], ACT.Ln, scale=scale, bias=m.cst[:, eps:eps + 1]).then_inc(logged, 1)
                act.wait_ge(logged, k + 1)
                nc.scalar.activation(rstd[:, k, :], rstd[:, k, :], ACT.Exp, scale=-0.5).then_inc(rooted, 1)

            def high(k):
                for a in range(2):
                    h = 2 * chunks[k][1] + a
                    act.wait_ge(scaled, (3 * KT if post else 0) + HALF * (h + 1))
                    nc.scalar.copy(m.p_hi[:, a * HALF:(a + 1) * HALF, cols(chunks[k][1])], tmp_pre[:, h % 3, :, :]).then_inc(hi_done, 1)

            n = len(chunks)
            squares(0)
            squares(1)
            for k in range(n):
                both = n == 6
                if both and 3 <= k < 5:
                    squares(k + 1)
                root(k)
                if both and k == 2:
                    squares(3)
                if k + 2 < 3:
                    squares(k + 2)
                if chunks[k][0] == "pre":
                    high(k)

        @block.vector
        def _(dve):
            def low(h):
                c, a = h // 2, h % 2
                dve.wait_ge(hi_done, h + 1)
                f = slice(a * HALF, (a + 1) * HALF)
                nc.vector.tensor_tensor(m.p_lo[:, f, cols(c)], tmp_pre[:, h % 3, :, :], m.p_hi[:, f, cols(c)].bitcast(F32), ALU.subtract).then_inc(lo_dve, 1)

            def scale(k):
                kind, c = chunks[k]
                dve.wait_ge(rooted, k + 1)
                for f in range(KT):
                    h = 2 * c + f // HALF
                    if kind == "pre":
                        if f % HALF == 0 and h >= 3:
                            wait_low(dve, h - 3)
                        if f == 5 and h == 3:
                            low(2)
                    x, gain = (post[0], post[1]) if kind == "post" else (m.resid, pre)
                    dst = x[:, f, cols(c)] if kind == "post" else tmp_pre[:, h % 3, f % HALF, :]
                    nc.vector.scalar_tensor_tensor(out=dst, in0=x[:, f, cols(c)], scalar=m.gain[:, gain + f:gain + f + 1],
                                                   in1=rstd[:, k, :], op0=ALU.mult, op1=ALU.mult).then_inc(scaled, 1)
                if kind == "post":
                    dve.wait_ge(scaled, KT * (c + 1))
                    nc.vector.tensor_tensor(m.resid[:, :, cols(c)], m.resid[:, :, cols(c)], post[0][:, :, cols(c)], ALU.add).then_inc(added, 1)

            for k in range(len(chunks)):
                scale(k)
            if pre is not None:
                low(5)

        if pre is not None:
            @block.gpsimd
            def _(pool):
                for h in (0, 1, 3, 4):
                    c, a = h // 2, h % 2
                    pool.wait_ge(hi_done, h + 1)
                    f = slice(a * HALF, (a + 1) * HALF)
                    nc.gpsimd.tensor_tensor(m.p_lo[:, f, cols(c)], tmp_pre[:, h % 3, :, :], m.p_hi[:, f, cols(c)].bitcast(F32),
                                            ALU.subtract).then_inc(lo_pool, 1)

        @block.tensor
        def _(pe):
            for k in range(len(chunks)):
                for a in range(2):
                    pe.wait_ge(squared, 2 * k + a + 1)
                    for f in range(HALF):
                        mm = nc.tensor.matmul(m.ps[:, k, 0:CH], m.cst[:, C_MEAN:C_MEAN + P], sq[:, a, f, :],
                                              start=(a == 0 and f == 0), stop=(a == 1 and f == HALF - 1))
                    mm.then_inc(summed, 1)


def ffn(nc, m, name, w_in, w_out):
    with ExitStack() as ctx:
        sem = semaphores(nc, ctx, name)
        w_in_full = [sem("raw_full0"), sem("raw_full1")]
        hi_done, lo_done, up_mm, down_mm = (sem(n) for n in ("w_hi", "w_lo", "up_mm", "down_mm"))
        silu_done, h_done, h_hi, h_split, down_added = (sem(n) for n in ("silu", "h", "h_hi", "h_split", "down_added"))
        hid_hi = ctx.enter_context(nc.sbuf_tensor(name + "hid_hi", [P, 2, 2, T], F32R))
        hid_lo = ctx.enter_context(nc.sbuf_tensor(name + "hid_lo", [P, 2, 2, T], F32R))
        silu = ctx.enter_context(nc.sbuf_tensor(name + "silu", [P, T], F32))
        hid = ctx.enter_context(nc.sbuf_tensor(name + "hid", [P, T], F32))
        block = ctx.enter_context(nc.Block())
        win = w_in.rearrange("o (f p) n -> p (o f) n", p=P)
        wout = w_out.rearrange("o (b t p) n -> p (o b) t n", p=P, t=2)

        def up_unit(b):
            return b * 6 - 2

        def down_unit(b):
            return b * 6 + 8

        LAST = 6 * BLK - 2

        def schedule(eng, up, down):
            up(0, 0, 0, True)
            up(1, 1, up_unit(1), True)
            down(0, 0, down_unit(0), True)
            with eng.Fori(1, BLK // 2) as i:
                for k in range(2):
                    up(2 * i + k, k, up_unit(2 * i + k), False)
                    down(2 * i + k - 1, 1 - k, down_unit(2 * i + k - 1), False)
            b = BLK - 1
            up(b, 0, up_unit(b), False)
            down(b - 1, 1, down_unit(b - 1), False)
            down(b, 0, LAST, False)

        @block.sync
        def _(sp):
            def load(unit, k, src, first):
                if not first:
                    sp.wait_ge(lo_done, unit - 1)
                sp.dma_start(m.w_raw[:, k, :].rearrange("p (a n) -> p a n", n=src.shape[-1]), src).then_inc(w_in_full[k], 16)

            def up(b, par, unit, peeled):
                for t in range(2):
                    for g in range(2):
                        load(unit + 2 * t + g, g, win[:, :, bass.ds(g * FF + (2 * b + t) * P, P)],
                             peeled and par == 0 and t == 0)

            def down(b, par, unit, peeled):
                for g in range(2):
                    load(unit + g, g, wout[:, bass.ds(b, 1), :, g * 512:(g + 1) * 512].rearrange("p o t n -> p (o t) n"), False)

            schedule(sp, up, down)

        @block.scalar
        def _(act):
            def high(unit, k):
                act.wait_ge(w_in_full[k], 8 * (unit - k) + 16)
                nc.scalar.copy(m.w_hi[:, k, :], m.w_raw[:, k, :]).then_inc(hi_done, 1)

            def up(b, par, unit, peeled):
                for t in range(2):
                    for g in range(2):
                        act.wait_ge(up_mm, 12 * b + 6 * t + 3 * g + 3)
                        high(unit + 2 * t + g + 2, g)
                        if g == 0:
                            for c in range(3):
                                if not (peeled and par == 0 and t == 0):
                                    act.wait_ge(h_done, 6 * b + 3 * t + c - 2)
                                nc.scalar.activation(silu[:, cols(c)], m.ps[:, c, 0:CH], ACT.Silu).then_inc(silu_done, 1)
                        else:
                            if not peeled and t == 0:
                                act.wait_ge(down_mm, 24 * b - 24)
                            for c in range(3):
                                act.wait_ge(h_done, 6 * b + 3 * t + c + 1)
                                nc.scalar.copy(hid_hi[:, par, t, cols(c)], hid[:, cols(c)]).then_inc(h_hi, 1)

            def down(b, par, unit, peeled):
                for g in range(2):
                    if isinstance(b, int) and b == BLK - 1:
                        return
                    act.wait_ge(down_mm, 24 * b + 12 * g + 12)
                    high(unit + g + 2, g)

            high(0, 0)
            high(1, 1)
            schedule(act, up, down)

        @block.vector
        def _(dve):
            def low(unit, k):
                dve.wait_ge(hi_done, unit + 1)
                nc.vector.tensor_tensor(m.w_lo[:, k, :], m.w_raw[:, k, :], m.w_hi[:, k, :].bitcast(F32),
                                        ALU.subtract).then_inc(lo_done, 1)

            def up(b, par, unit, peeled):
                for t in range(2):
                    first = peeled and par == 0 and t == 0
                    low(unit + 2 * t + 2, 0)
                    low(unit + 2 * t + 3, 1)
                    for c in range(3):
                        dve.wait_ge(up_mm, 12 * b + 6 * t + 3 + c + 1)
                        dve.wait_ge(silu_done, 6 * b + 3 * t + c + 1)
                        if not first:
                            dve.wait_ge(h_split, 6 * b + 3 * t + c - 2)
                        nc.vector.tensor_tensor(hid[:, cols(c)], silu[:, cols(c)], m.ps[:, 3 + c, 0:CH], ALU.mult).then_inc(h_done, 1)

            def down(b, par, unit, peeled):
                for o in range(KT):
                    for c in range(3):
                        dve.wait_ge(down_mm, 24 * b + 3 * o + c + 1)
                        bank = 3 * (o % 2) + c
                        if peeled:
                            nc.vector.tensor_copy(m.acc[:, o, cols(c)], m.ps[:, bank, 0:CH]).then_inc(down_added, 1)
                        else:
                            dve.wait_ge(down_added, 24 * b + 3 * o + c - 23)
                            nc.vector.tensor_tensor(m.acc[:, o, cols(c)], m.acc[:, o, cols(c)], m.ps[:, bank, 0:CH],
                                                    ALU.add).then_inc(down_added, 1)
                    if o % 4 == 3 and not (isinstance(b, int) and b == BLK - 1):
                        low(unit + o // 4 + 2, o // 4)

            low(0, 0)
            low(1, 1)
            schedule(dve, up, down)

        @block.gpsimd
        def _(pool):
            def up(b, par, unit, peeled):
                for t in range(2):
                    for c in range(3):
                        pool.wait_ge(h_hi, 6 * b + 3 * t + c + 1)
                        nc.gpsimd.tensor_tensor(hid_lo[:, par, t, cols(c)], hid[:, cols(c)],
                                                hid_hi[:, par, t, cols(c)].bitcast(F32), ALU.subtract).then_inc(h_split, 1)

            def down(b, par, unit, peeled):
                pass

            schedule(pool, up, down)

        @block.tensor
        def _(pe):
            def up(b, par, unit, peeled):
                for t in range(2):
                    for g in range(2):
                        pe.wait_ge(lo_done, unit + 2 * t + g + 1)
                        for c in range(3):
                            if t == 1:
                                pe.wait_ge((silu_done, h_done)[g], 6 * b + c + 1)
                            elif not peeled:
                                pe.wait_ge(down_added, 24 * b - 24 - 6 + 3 * g + c + 1)
                            elif par == 1:
                                pe.wait_ge((silu_done, h_done)[g], 6 * b - 3 + c + 1)
                            for f in range(KT):
                                w = slice(f * P, (f + 1) * P)
                                for n, (a, x) in enumerate(((m.w_hi, m.p_hi), (m.w_hi, m.p_lo), (m.w_lo, m.p_hi))):
                                    mm = nc.tensor.matmul(m.ps[:, 3 * g + c, 0:CH], a[:, g, w], x[:, f, cols(c)],
                                                          start=(f == 0 and n == 0), stop=(f == KT - 1 and n == 2))
                            mm.then_inc(up_mm, 1)

            def down(b, par, unit, peeled):
                pe.wait_ge(h_split, 6 * b + 6)
                for o in range(KT):
                    g = o // 4
                    if o % 4 == 0:
                        pe.wait_ge(lo_done, unit + g + 1)
                    for c in range(3):
                        if o >= 2:
                            pe.wait_ge(down_added, 24 * b + 3 * (o - 2) + c + 1)
                        elif par == 0 and not peeled and isinstance(b, int):
                            pe.wait_ge(down_added, 24 * b + 3 * (o - 2) + c + 1)
                        else:
                            pe.wait_ge((silu_done, h_done)[o], 6 * b + 6 + 3 + c + 1)
                        for t in range(2):
                            w = slice(t * 512 + (o % 4) * P, t * 512 + (o % 4) * P + P)
                            for n, (a, x) in enumerate(((m.w_hi, hid_hi), (m.w_hi, hid_lo), (m.w_lo, hid_hi))):
                                mm = nc.tensor.matmul(m.ps[:, 3 * (o % 2) + c, 0:CH], a[:, g, w], x[:, par, t, cols(c)],
                                                      start=(t == 0 and n == 0), stop=(t == 1 and n == 2))
                        mm.then_inc(down_mm, 1)

            schedule(pe, up, down)


def store_tokens(nc, m, y_prompt, y_sample):
    with ExitStack() as ctx:
        sem = semaphores(nc, ctx, "")
        turned, moved = sem("st_turned"), sem("st_moved")
        stored = [sem("st_stored0"), sem("st_stored1")]
        rows = ctx.enter_context(nc.sbuf_tensor("out_rows", [P, 2, D], F32))
        block = ctx.enter_context(nc.Block())
        yp = y_prompt.rearrange("o (t p) d -> (o t) p d", p=P)

        @block.tensor
        def _(pe):
            for i in range(TT + 1):
                n = P if i < TT else NS
                if i >= 2:
                    pe.wait_ge(moved, i - 1)
                for f in range(KT):
                    mm = nc.tensor.transpose(m.ps[0:n, 2 * (i % 2) + f // 4, (f % 4) * P:(f % 4 + 1) * P],
                                             m.resid[:, f, i * P:i * P + n], m.cst[:, C_ID:C_ID + P])
                mm.then_inc(turned, 1)

        @block.vector
        def _(dve):
            for i in range(TT + 1):
                n = P if i < TT else NS
                dve.wait_ge(turned, i + 1)
                if i >= 2:
                    dve.wait_ge(stored[i % 2], 16 * (i // 2))
                k = i % 2
                nc.vector.tensor_copy(rows[0:n, k, :].rearrange("p (b f) -> p b f", b=2), m.ps[0:n, 2 * k:2 * k + 2, :]).then_inc(moved, 1)

        @block.sync
        def _(sp):
            for i in range(TT + 1):
                sp.wait_ge(moved, i + 1)
                if i < TT:
                    sp.dma_start(yp[i], rows[:, i % 2, :]).then_inc(stored[i % 2], 16)
                else:
                    sp.dma_start(y_sample.rearrange("b l d -> (b l) d"), rows[0:NS, 0, :]).then_inc(stored[0], 16)
            sp.wait_ge(stored[0], 16 * 5)
            sp.wait_ge(stored[1], 16 * 4)


def attention_heads(nc, m, w_in, o_dram, k_prompt, v_prompt, k_sample, v_sample):
    G = 9
    fills = []
    for i in range(TT):
        for j in range(0, i + 1, 4):
            fills.append(("prob", i, j))
        fills.append(("value", i, 0))
    for n in range(3):
        fills.append(("key_rows", n, 0))
    for n in range(3):
        fills.append(("value_rows", n, 0))
    for n in range(2):
        fills.append(("out", n, 0))
    NF = len(fills)
    order = {f: n for n, f in enumerate(fills)}
    by_act = {f: sum(g[0] in ("value", "key_rows") for g in fills[:n]) for f, n in order.items()}
    by_dve = {f: n - by_act[f] for f, n in order.items()}
    NA = sum(f[0] in ("value", "key_rows") for f in fills)
    ND = NF - NA
    with ExitStack() as ctx:
        sem = semaphores(nc, ctx, "at_")
        sb = lambda n, s, d=F32: ctx.enter_context(nc.sbuf_tensor("at_" + n, s, d))
        raw_full = [sem("raw_full0"), sem("raw_full1")]
        (hi_done, lo_done, proj_mm, scores_mm, filled, moved_act, moved_dve) = (
            sem(n) for n in ("w_hi", "w_lo", "proj_mm", "scores", "filled", "moved_act", "moved_dve"))
        (rope_in, cos_done, rot_done, sin_done, roped, v_raw_done, saved, saved_v) = (
            sem(n) for n in ("rope_in", "cos_done", "rot_done", "sin_done", "roped", "v_raw", "saved", "saved_v"))
        (masked, neg_max, exp_done, inv_done, ratio_done, mixed) = (
            sem(n) for n in ("masked", "neg_max", "exp", "inv", "ratio", "mixed"))
        (scaled, out_ln, out_rstd, out_normed, k_out, o_out) = (
            sem(n) for n in ("scaled", "out_ln", "out_rstd", "out_normed", "k_out", "o_out"))
        v_out = [sem("v_out0"), sem("v_out1")]
        rope = sb("rope", [P, NROPE])
        qk = sb("qk", [P, 2, 2, T])
        v_raw = sb("v_raw", [P, T])
        cosx = sb("cosx", [P, 2, CH])
        rotx = sb("rotx", [P, 2, CH])
        k_rows = sb("k_rows", [P, TT + 1, P])
        v_rows = sb("v_rows", [P, 2, TT + 1, P])
        pr = sb("prob", [P, 2, 2, LP])
        pt = sb("prob_t", [P, 2, TT, P])
        nmax = sb("nmax", [P, 2, 2])
        den = sb("den", [P, 2, 2])
        inv = sb("inv", [P, 2, 2])
        ratio = sb("ratio", [P, 2])
        o_rows = sb("o_rows", [P, TT, P])
        o_sq = sb("o_sq", [P, P])
        o_ss = sb("o_ss", [P, 2, TT])
        o_ln = sb("o_ln", [P, TT])
        o_rs = sb("o_rs", [P, TT])
        o_nrm = sb("o_nrm", [P, TT, P])
        o_t = sb("o_t", [P, LP])
        block = ctx.enter_context(nc.Block())
        win = w_in.rearrange("o (f p) n -> p (o f) n", p=P)
        ident = m.cst[:, C_ID:C_ID + P]

        def schedule(eng, products, head):
            products(0)
            head(0, 0, True)
            head(1, 1, True)
            with eng.Fori(1, H // 2 - 1) as i:
                head(2 * i, 0, True)
                head(2 * i + 1, 1, True)
            head(H - 2, 0, True)
            head(H - 1, 1, False)

        def unit_parity(par, u):
            return (par + u) % 2

        @block.sync
        def _(sp):
            sp.dma_start(rope[:, :], m.d_rope).then_inc(rope_in, 16)

            def loads(h, par):
                for u in range(3):
                    k = unit_parity(par, u)
                    if not (isinstance(h, int) and h == 0 and u < 2):
                        sp.wait_ge(lo_done, 3 * h + u - 1)
                    sp.dma_start(m.w_raw[:, k, :].rearrange("p (f n) -> p f n", n=P),
                                 win[:, :, bass.ds(u * D + h * P, P)]).then_inc(raw_full[k], 16)

            schedule(sp, lambda h: loads(h, 0), lambda h, par, more: loads(h + 1, 1 - par) if more else None)

        def split_args(h, par, u):
            k = unit_parity(par, u)
            n = 3 * h + u
            return n, k, 8 * (n - k) + 16

        @block.scalar
        def _(act):
            def high(h, par, u):
                n, k, full = split_args(h, par, u)
                act.wait_ge(raw_full[k], full)
                nc.scalar.copy(m.w_hi[:, k, :], m.w_raw[:, k, :]).then_inc(hi_done, 1)

            def take(h, par, g, last):
                u, c, bank = g // 3, g % 3, (par + g) % 2
                act.wait_ge(proj_mm, G * h + g + 1)
                if u < 2:
                    n = 6 * h + g
                    act.wait_ge(cos_done, n + 1)
                    if not (isinstance(h, int) and h == 0 and g < 2):
                        act.wait_ge(roped, n - 1)
                    for q in range(4):
                        dst = rotx[32 * q:32 * q + 32, g % 2, :]
                        src = m.ps[32 * (q ^ 1):32 * (q ^ 1) + 32, bank, 0:CH]
                        ins = nc.scalar.mul(dst, src, HD ** -0.5 if u == 0 else 1.0)
                        ins.then_inc(rot_done, 1)
                else:
                    if not (isinstance(h, int) and h == 0):
                        act.wait_ge(filled, NF * (h - 1) + 6)
                    nc.scalar.copy(v_raw[:, cols(c)], m.ps[:, bank, 0:CH]).then_inc(v_raw_done, 1)
                if c == 2 and not (last and u >= 1):
                    high(h + (u + 2) // 3, (par + (u + 2) // 3) % 2, (u + 2) % 3)

            def rows(h, par):
                for n in range(3):
                    f = ("key_rows", n, 0)
                    act.wait_ge(filled, NF * (h - 1) + 6 + order[f] + 1 if not isinstance(h, int) or h > 0 else n + 1)
                    if n == 0:
                        if not (isinstance(h, int) and h == 0):
                            act.wait_ge(k_out, 32 * h)
                    b = 6 + (order[f] % 2)
                    if n < 2:
                        nc.scalar.copy(k_rows[:, 4 * n:4 * n + 4, :], m.ps[:, b, :].rearrange("p (t d) -> p t d", d=P)).then_inc(moved_act, 1)
                    else:
                        nc.scalar.copy(k_rows[0:NS, TT, :], m.ps[0:NS, b, 0:P]).then_inc(moved_act, 1)

            def products(h):
                high(0, 0, 0)
                high(0, 0, 1)
                for g in range(G):
                    take(0, 0, g, False)
                rows(0, 0)

            def head(h, par, more):
                fb, ab = NF * h + 6, NA * h + 3

                def value(i):
                    f = ("value", i, 0)
                    act.wait_ge(filled, fb + order[f] + 1)
                    act.wait_ge(inv_done, TT * h + i + 1)
                    if i == 0 and not (isinstance(h, int) and h == 0):
                        act.wait_ge(out_normed, h)
                    nc.scalar.activation(o_rows[:, i, :], m.ps[:, 6 + order[f] % 2, 0:P], ACT.Copy,
                                         scale=inv[:, i % 2, 0:1]).then_inc(moved_act, 1)
                    act.wait_ge(moved_act, ab + by_act[f] + 1)
                    nc.scalar.activation(o_sq[:, :], o_rows[:, i, :], ACT.Square, accum_out=o_ss[:, 0, i:i + 1]).then_inc(scaled, 1)

                for i in range(TT + 1):
                    if i < TT:
                        for a in range(2):
                            act.wait_ge(neg_max, 2 * TT * h + 2 * i + a + 1)
                            if i >= 2:
                                act.wait_ge(filled, fb + order[("value", i - 2, 0)])
                            elif not (isinstance(h, int) and h == 0):
                                act.wait_ge(filled, NF * (h - 1) + 6 + order[("value", TT - 2 + i, 0)])
                            nc.scalar.activation(pr[:, i % 2, a, 0:(i + 1) * P],
                                                 m.ps[:, 2 + 2 * a:4 + 2 * a, :].rearrange("p b k -> p (b k)")[:, 0:(i + 1) * P],
                                                 ACT.Exp, bias=nmax[:, i % 2, a:a + 1],
                                                 accum_out=den[:, i % 2, a:a + 1]).then_inc(exp_done, 1)
                    if more:
                        take(h + 1, 1 - par, i, isinstance(h, int) and h == H - 2)
                    if i >= 1:
                        value(i - 1)
                if more:
                    rows(h + 1, 1 - par)
                act.wait_ge(scaled, TT * h + TT)
                nc.scalar.activation(o_ln[:, :], o_ss[:, 0, :], ACT.Ln, scale=1.0 / P, bias=m.cst[:, C_EPS:C_EPS + 1]).then_inc(out_ln, 1)
                act.wait_ge(out_ln, h + 1)
                nc.scalar.activation(o_rs[:, :], o_ln[:, :], ACT.Exp, scale=-0.5).then_inc(out_rstd, 1)

            schedule(act, products, head)

        @block.vector
        def _(dve):
            def low(h, par, u):
                n, k, _ = split_args(h, par, u)
                dve.wait_ge(hi_done, n + 1)
                nc.vector.tensor_tensor(m.w_lo[:, k, :], m.w_raw[:, k, :], m.w_hi[:, k, :].bitcast(F32),
                                        ALU.subtract).then_inc(lo_done, 1)

            def take(h, par, g, last):
                u, c, bank = g // 3, g % 3, (par + g) % 2
                if u < 2:
                    dve.wait_ge(proj_mm, G * h + g + 1)
                    if not (isinstance(h, int) and h == 0 and g < 2):
                        dve.wait_ge(roped, 6 * h + g - 1)
                    nc.vector.scalar_tensor_tensor(out=cosx[:, g % 2, :], in0=m.ps[:, bank, 0:CH],
                                                   scalar=HD ** -0.5 if u == 0 else 1.0, in1=rope[:, cols(c)],
                                                   op0=ALU.mult, op1=ALU.mult).then_inc(cos_done, 1)
                if c == 2 and not (last and u >= 1):
                    low(h + (u + 2) // 3, (par + (u + 2) // 3) % 2, (u + 2) % 3)

            def rows(h, par):
                for n in range(3):
                    f = ("value_rows", n, 0)
                    dve.wait_ge(filled, NF * (h - 1) + 6 + order[f] + 1 if not isinstance(h, int) or h > 0 else n + 4)
                    if n == 0 and not (isinstance(h, int) and h < 2):
                        dve.wait_ge(v_out[par], 16 * (h - par))
                        dve.wait_ge(saved_v, h - 1)
                    b = 6 + (order[f] % 2)
                    if n < 2:
                        nc.vector.tensor_scalar(v_rows[:, par, 4 * n:4 * n + 4, :], m.ps[:, b, :].rearrange("p (t d) -> p t d", d=P),
                                                1.0, None, ALU.mult).then_inc(moved_dve, 1)
                    else:
                        nc.vector.tensor_scalar(v_rows[0:NS, par, TT, :], m.ps[0:NS, b, 0:P], 1.0, None, ALU.mult).then_inc(moved_dve, 1)

            def products(h):
                dve.wait_ge(rope_in, 16)
                low(0, 0, 0)
                low(0, 0, 1)
                for g in range(G):
                    take(0, 0, g, False)
                rows(0, 0)

            def head(h, par, more):
                fb, db = NF * h + 6, ND * h + 3
                for i in range(TT + 1):
                    if i < TT:
                        for a in range(2):
                            n = 2 * TT * h + 2 * i + a
                            s = m.ps[:, 2 + 2 * a:4 + 2 * a, :].rearrange("p b k -> p (b k)")
                            dve.wait_ge(scores_mm, n + 1)
                            nc.vector.tensor_tensor(s[:, i * P:(i + 1) * P], s[:, i * P:(i + 1) * P], m.cst[:, C_CAUS:C_CAUS + P],
                                                    ALU.add).then_inc(masked, 1)
                            dve.wait_ge(masked, n + 1)
                            nc.vector.tensor_reduce(nmax[:, i % 2, a:a + 1], s[:, 0:(i + 1) * P], AX.X, ALU.max,
                                                    negate=True).then_inc(neg_max, 1)
                    if i >= 1:
                        for j in range(0, i, 4):
                            f = ("prob", i - 1, j)
                            w = min(4, i - j)
                            dve.wait_ge(filled, fb + order[f] + 1)
                            nc.vector.tensor_scalar(pt[:, (i - 1) % 2, j:j + w, :],
                                                    m.ps[:, 6 + order[f] % 2, 0:w * P].rearrange("p (t d) -> p t d", d=P),
                                                    1.0, None, ALU.mult).then_inc(moved_dve, 1)
                    if i < TT:
                        dve.wait_ge(exp_done, 2 * TT * h + 2 * i + 2)
                        wait(dve, scaled, TT * h + i - 1)
                        nc.vector.reciprocal(inv[:, i % 2, :], den[:, i % 2, :]).then_inc(inv_done, 1)
                        dve.wait_ge(inv_done, TT * h + i + 1)
                        nc.vector.scalar_tensor_tensor(out=ratio[:, i % 2:i % 2 + 1], in0=inv[:, i % 2, 1:2], scalar=den[:, i % 2, 0:1],
                                                       in1=m.lam[:, 1:2], op0=ALU.mult, op1=ALU.mult).then_inc(ratio_done, 1)
                        dve.wait_ge(ratio_done, TT * h + i + 1)
                        nc.vector.scalar_tensor_tensor(out=pr[:, i % 2, 0, 0:(i + 1) * P], in0=pr[:, i % 2, 1, 0:(i + 1) * P],
                                                       scalar=ratio[:, i % 2:i % 2 + 1], in1=pr[:, i % 2, 0, 0:(i + 1) * P],
                                                       op0=ALU.mult, op1=ALU.add).then_inc(mixed, 1)
                    if more:
                        take(h + 1, 1 - par, i, isinstance(h, int) and h == H - 2)
                if more:
                    rows(h + 1, 1 - par)
                dve.wait_ge(out_rstd, h + 1)
                if not (isinstance(h, int) and h == 0):
                    dve.wait_ge(filled, fb)
                nc.vector.tensor_tensor(o_nrm[:, :, :], o_rows[:, :, :], o_rs[:, :].rearrange("p (t o) -> p t o", o=1).to_broadcast([P, TT, P]),
                                        ALU.mult).then_inc(out_normed, 1)
                for n in range(2):
                    f = ("out", n, 0)
                    dve.wait_ge(filled, fb + order[f] + 1 - (0 if more else 6))
                    if n == 0 and not (isinstance(h, int) and h == 0):
                        dve.wait_ge(o_out, 16 * h)
                    nc.vector.tensor_scalar(o_t[:, n * 512:(n + 1) * 512], m.ps[:, 6 + order[f] % 2, :], m.gain[:, 6 * KT:6 * KT + 1],
                                            1.0 - LAM_INIT, ALU.mult, ALU.mult).then_inc(moved_dve, 1)

            schedule(dve, products, head)

        @block.gpsimd
        def _(pool):
            kp = k_prompt.rearrange("o b (t p) h d -> p (o b t) h d", p=P)
            vp = v_prompt.rearrange("o b (t p) h d -> p (o b t) h d", p=P)
            ks = k_sample.rearrange("o b l h d -> (o b l) h d")
            vs = v_sample.rearrange("o b l h d -> (o b l) h d")

            def rotate(h, par, g):
                u, c = g // 3, g % 3
                n = 6 * h + g
                pool.wait_ge(rot_done, 4 * n + 4)
                nc.gpsimd.tensor_tensor(rotx[:, g % 2, :], rotx[:, g % 2, :], rope[:, T + c * CH:T + (c + 1) * CH], ALU.mult).then_inc(sin_done, 1)
                pool.wait_ge(sin_done, n + 1)
                pool.wait_ge(cos_done, n + 1)
                if g == 0 and not (isinstance(h, int) and h < 2):
                    pool.wait_ge(scores_mm, 2 * TT * (h - 1))
                    pool.wait_ge(saved, 2 * h - 2)
                nc.gpsimd.tensor_tensor(qk[:, par, u, cols(c)], rotx[:, g % 2, :], cosx[:, g % 2, :], ALU.add).then_inc(roped, 1)

            def outputs(h, par):
                pool.wait_ge(roped, 6 * h + 6)
                nc.gpsimd.tensor_copy(m.q_s[:, bass.ds(h, 1), :].rearrange("p o t -> p (o t)"), qk[:, par, 0, LP:T]).then_inc(saved, 1)
                nc.gpsimd.tensor_copy(m.k_s[:, bass.ds(h, 1), :].rearrange("p o t -> p (o t)"), qk[:, par, 1, LP:T]).then_inc(saved, 1)
                pool.wait_ge(moved_act, NA * h + 3)
                pool.dma_start(kp[:, :, bass.ds(h, 1), :].rearrange("p t o d -> p (t o) d"), k_rows[:, 0:TT, :]).then_inc(k_out, 16)
                pool.dma_start(ks[:, bass.ds(h, 1), :].rearrange("p o d -> p (o d)"), k_rows[0:NS, TT, :]).then_inc(k_out, 16)
                pool.wait_ge(moved_dve, ND * h + 3)
                nc.gpsimd.tensor_copy(m.v_s[0:NS, bass.ds(h, 1), :].rearrange("p o t -> p (o t)"), v_rows[0:NS, par, TT, :]).then_inc(saved_v, 1)
                pool.dma_start(vp[:, :, bass.ds(h, 1), :].rearrange("p t o d -> p (t o) d"), v_rows[:, par, 0:TT, :]).then_inc(v_out[par], 16)
                pool.dma_start(vs[:, bass.ds(h, 1), :].rearrange("p o d -> p (o d)"), v_rows[0:NS, par, TT, :]).then_inc(v_out[par], 16)

            def products(h):
                pool.wait_ge(rope_in, 16)
                for g in range(6):
                    rotate(0, 0, g)
                outputs(0, 0)

            def head(h, par, more):
                if more:
                    for g in range(6):
                        rotate(h + 1, 1 - par, g)
                    outputs(h + 1, 1 - par)
                pool.wait_ge(moved_dve, ND * h + ND + (3 if more else 0))
                pool.dma_start(o_dram[bass.ds(h, 1), :, 0:LP].rearrange("o p t -> (o p) t"), o_t[:, :]).then_inc(o_out, 16)

            schedule(pool, products, head)
            pool.wait_ge(k_out, 32 * H)
            for par in range(2):
                pool.wait_ge(v_out[par], 16 * H)
            pool.wait_ge(o_out, 16 * H)

        @block.tensor
        def _(pe):
            pe.wait_ge(rope_in, 16)

            def group(h, par, g):
                u, c, bank = g // 3, g % 3, (par + g) % 2
                first = isinstance(h, int) and h == 0
                if c == 0:
                    pe.wait_ge(lo_done, 3 * h + u + 1)
                if g in (0, 1):
                    if not first:
                        pe.wait_ge(v_raw_done, 3 * h - 1 + g)
                elif g < 8:
                    pe.wait_ge(rot_done, 4 * (6 * h + g - 1))
                    pe.wait_ge(cos_done, 6 * h + g - 1)
                else:
                    pe.wait_ge(v_raw_done, 3 * h + 1)
                for f in range(KT):
                    w = slice(f * P, (f + 1) * P)
                    for n, (a, x) in enumerate(((m.w_hi, m.p_hi), (m.w_hi, m.p_lo), (m.w_lo, m.p_hi))):
                        mm = nc.tensor.matmul(m.ps[:, bank, 0:CH], a[:, unit_parity(par, u), w], x[:, f, cols(c)],
                                              start=(f == 0 and n == 0), stop=(f == KT - 1 and n == 2))
                mm.then_inc(proj_mm, 1)

            def fill_free(h, fill, base_f, base_a, base_d, none=False):
                n = order[fill]
                if n >= 2:
                    g = fills[n - 2]
                    if g[0] in ("value", "key_rows"):
                        pe.wait_ge(moved_act, base_a + by_act[g] + 1)
                    else:
                        pe.wait_ge(moved_dve, base_d + by_dve[g] + 1)
                elif not none:
                    pe.wait_ge(moved_dve, base_d - 1 + n)

            def rows(h, par):
                first = isinstance(h, int) and h == 0
                bf, ba, bd = (NF * (h - 1) + 6, NA * (h - 1) + 3, ND * (h - 1) + 3) if not first else (0, 0, 0)
                for kind in ("key_rows", "value_rows"):
                    for n in range(3):
                        f = (kind, n, 0)
                        if not first:
                            fill_free(h, f, bf, ba, bd)
                        elif kind == "value_rows" or n == 2:
                            k = n + (0 if kind == "key_rows" else 3) - 2
                            pe.wait_ge(moved_act, k + 1) if k < 3 else pe.wait_ge(moved_dve, k - 2)
                        if n == 0:
                            pe.wait_ge(roped, 6 * h + 6) if kind == "key_rows" else pe.wait_ge(v_raw_done, 3 * h + 3)
                        b = 6 + order[f] % 2
                        src = qk[:, par, 1, :] if kind == "key_rows" else v_raw[:, :]
                        if n < 2:
                            for t in range(4):
                                mm = nc.tensor.transpose(m.ps[:, b, t * P:(t + 1) * P], src[:, (4 * n + t) * P:(4 * n + t + 1) * P], ident)
                        else:
                            mm = nc.tensor.transpose(m.ps[0:NS, b, 0:P], src[:, LP:T], ident)
                        mm.then_inc(filled, 1)

            def products(h):
                for g in range(G):
                    group(0, 0, g)
                rows(0, 0)

            def head(h, par, more):
                first = isinstance(h, int) and h == 0
                bf, ba, bd = NF * h + 6, NA * h + 3, ND * h + 3

                def scores(i):
                    for a in range(2):
                        wait(pe, exp_done, 2 * TT * h + 2 * i + a - 1)
                        for k in range(0, (i + 1) * P, 512):
                            w = min(512, (i + 1) * P - k)
                            mm = nc.tensor.matmul(m.ps[:, 2 + 2 * a + k // 512, 0:w], qk[64 * a:64 * a + 64, par, 0, i * P:(i + 1) * P],
                                                  qk[64 * a:64 * a + 64, par, 1, k:k + w], start=True, stop=True)
                        mm.then_inc(scores_mm, 1)

                def turn(i):
                    pe.wait_ge(mixed, TT * h + i + 1)
                    for j in range(0, i + 1, 4):
                        f = ("prob", i, j)
                        fill_free(h, f, bf, ba, bd)
                        w = min(4, i + 1 - j)
                        for t in range(w):
                            mm = nc.tensor.transpose(m.ps[:, 6 + order[f] % 2, t * P:(t + 1) * P], pr[:, i % 2, 0, (j + t) * P:(j + t + 1) * P], ident)
                        mm.then_inc(filled, 1)

                def values(i):
                    f = ("value", i, 0)
                    fill_free(h, f, bf, ba, bd)
                    pe.wait_ge(moved_dve, bd + by_dve[("prob", i, 4 if i >= 4 else 0)] + 1)
                    for j in range(i + 1):
                        mm = nc.tensor.matmul(m.ps[:, 6 + order[f] % 2, 0:P], pt[:, i % 2, j, :], v_rows[:, par, j, :],
                                              start=(j == 0), stop=(j == i))
                    mm.then_inc(filled, 1)

                for i in range(TT + 1):
                    if i < TT:
                        scores(i)
                    if i >= 1:
                        turn(i - 1)
                    if more:
                        group(h + 1, 1 - par, i)
                    if i >= 1:
                        values(i - 1)
                if more:
                    rows(h + 1, 1 - par)
                pe.wait_ge(out_normed, h + 1)
                for n in range(2):
                    f = ("out", n, 0)
                    if more:
                        fill_free(h, f, bf, ba, bd)
                    else:
                        g = ("prob", TT - 1, 4) if n == 0 else ("value", TT - 1, 0)
                        pe.wait_ge(moved_dve, bd + by_dve[g] + 1) if n == 0 else pe.wait_ge(moved_act, ba + by_act[g] + 1)
                    for t in range(4):
                        mm = nc.tensor.transpose(m.ps[:, 6 + order[f] % 2, t * P:(t + 1) * P], o_nrm[:, 4 * n + t, :], ident)
                    mm.then_inc(filled, 1)

            schedule(pe, products, head)


def attention_sample(nc, m, cache_k, cache_v, page_table, o_dram):
    HG = H // 2
    W = HG * P
    FILLS = HG * NPAGE // 4
    COMB, TURN = 32, 192
    with ExitStack() as ctx:
        sem = semaphores(nc, ctx, "sa_")
        sb = lambda n, s, d=F32: ctx.enter_context(nc.sbuf_tensor("sa_" + n, s, d))
        table_in, q_zero, q_placed, q_staged, stored = (sem(n) for n in ("table_in", "q_zero", "q_placed", "q_staged", "stored"))
        k_full, v_full = [sem("k_full0"), sem("k_full1")], [sem("v_full0"), sem("v_full1")]
        turned, kt_act, kt_dve, scored, masked, max_two, neg_max = (
            sem(n) for n in ("turned", "kt_act", "kt_dve", "scored", "masked", "max_two", "neg_max"))
        exp_done, den_done, inv_done, comb_done, combined, pt_done, valued, o_done, row_done, o_turned = (
            sem(n) for n in ("exp", "den", "inv", "comb", "combined", "pt", "valued", "o", "row", "o_turned"))
        sq_done, summed, ln_done, rs_done, normed, gained = (sem(n) for n in ("sq", "summed", "ln", "rs", "normed", "gained"))
        table = sb("table", [1, NB * NPAGE], I32)
        kb = sb("k", [P, 2, NPAGE, W])
        vb = sb("v", [P, 2, NPAGE, W])
        kt = sb("kt", [P, HG, PAST])
        qz = sb("q_zeroed", [P, H, NB, 32])
        qst = sb("q_staged", [P, 2, HG, 32])
        pr = sb("prob", [P, 2, PAST + NS])
        sn = sb("scores_new", [P, NS + 2])
        nmax = sb("nmax", [P, 2])
        den = sb("den", [P, 2])
        inv = sb("inv", [P, 2])
        cmb = sb("comb", [P, 2, 16])
        pt = sb("prob_t", [P, NPAGE, 16])
        ptn = sb("prob_t_new", [NS, 16])
        o_row = m.w_raw[0:HG * LS, 1, 512:512 + W]
        o_s = sb("o", [P, H, NS])
        o_q, o_n = m.w_raw[:, 0, 0:H * NS], m.w_raw[:, 0, 512:512 + H * NS]
        rs = m.w_raw[:, 1, 0:2 * H * NS].rearrange("p (n t) -> p n t", n=2)
        block = ctx.enter_context(nc.Block())
        ident = m.cst[:, C_ID:C_ID + P]
        ck = cache_k.rearrange("o n p h d -> (o n) p (h d)")
        cv = cache_v.rearrange("o n p h d -> (o n) p (h d)")

        def schedule(eng, step):
            step(0, 0)
            step(0, 1)
            with eng.Fori(1, NB) as b:
                for g in range(2):
                    step(b, g)
            step(NB, 0)
            step(NB, 1)

        def stages(b, g):
            whole = not isinstance(b, int)
            n = None if whole else 2 * b + g
            return (whole or n < 2 * NB, whole or 1 <= n <= 2 * NB, whole or 2 <= n,
                    (b, 0) if g else (b - 1, 1), (b - 1, g))

        @block.sync
        def _(sp):
            sp.dma_start(table[0:1, :], page_table.rearrange("(o b) n -> o (b n)", o=1)).then_inc(table_in, 16)
            sp.wait_ge(table_in, 16)

            def step(b, g):
                if not stages(b, g)[0]:
                    return
                first = isinstance(b, int) and b == 0
                pages = [sp.value_load(table[0:1, bass.ds(b * NPAGE + n, 1)], min_val=0, max_val=ck.shape[0] - 1) for n in range(NPAGE)]
                if not first:
                    sp.wait_ge(turned, FILLS * (2 * b + g - 1))
                for n, page in enumerate(pages):
                    sp.dma_start(kb[:, g, n, :], ck[bass.ds(page, 1), :, g * W:(g + 1) * W].rearrange("o p w -> (o p) w")).then_inc(k_full[g], 16)
                if not first:
                    sp.wait_ge(valued, 2 * b + g - 1)
                for n, page in enumerate(pages):
                    sp.dma_start(vb[:, g, n, :], cv[bass.ds(page, 1), :, g * W:(g + 1) * W].rearrange("o p w -> (o p) w")).then_inc(v_full[g], 16)

            schedule(sp, step)
            sp.wait_ge(gained, H)
            sp.dma_start(o_dram[:, :, LP:T].rearrange("h p t -> p h t"), o_s[:, :, :]).then_inc(stored, 16)
            sp.wait_ge(stored, 16)

        @block.scalar
        def _(act):
            def step(b, g):
                n = 2 * b + g
                new, combining, _, _, _ = stages(b, g)
                if new:
                    for f in range(0, FILLS, 2):
                        act.wait_ge(turned, FILLS * n + f + 1)
                        nc.scalar.copy(kt[:, f // 2, 0:512], m.ps[:, f % 4, :]).then_inc(kt_act, 1)
                    act.wait_ge(neg_max, n + 1)
                    wait(act, combined, n - 1)
                    nc.scalar.activation(pr[:, g, 0:PAST], m.ps[:, 4:6, :].rearrange("p b k -> p (b k)"), ACT.Exp,
                                         bias=nmax[:, g:g + 1], accum_out=den[:, 0:1]).then_inc(exp_done, 1)
                    nc.scalar.activation(pr[:, g, PAST:PAST + NS], sn[:, 0:NS], ACT.Exp, bias=nmax[:, g:g + 1],
                                         accum_out=den[:, 1:2]).then_inc(exp_done, 1)
                if combining:
                    act.wait_ge(valued, n)
                    wait(act, o_turned, n - 1)
                    nc.scalar.copy(o_row[:, :], m.ps[0:HG * LS, 6, :]).then_inc(row_done, 1)

            schedule(act, step)
            act.wait_ge(summed, 1)
            nc.scalar.activation(rs[:, 0, :], m.ps[:, 0, 0:H * NS], ACT.Ln, scale=1.0 / P, bias=m.cst[:, C_EPS:C_EPS + 1]).then_inc(ln_done, 1)
            act.wait_ge(ln_done, 1)
            nc.scalar.activation(rs[:, 1, :], rs[:, 0, :], ACT.Exp, scale=-0.5).then_inc(rs_done, 1)

        @block.gpsimd
        def _(pool):
            nc.gpsimd.memset(qz[:, :, :, :], 0.0).then_inc(q_zero, 1)

        @block.vector
        def _(dve):
            dve.wait_ge(q_zero, 1)
            for a in range(2):
                nc.vector.tensor_copy(qz[64 * a:64 * a + 64, :, :, LS * a:LS * a + LS],
                                      m.q_s[64 * a:64 * a + 64, :, :].rearrange("p h (b q) -> p h b q", q=LS)).then_inc(q_placed, 1)
            dve.wait_ge(q_placed, 2)

            def stage(b, g, first):
                if not first:
                    dve.wait_ge(scored, 2 * b + g - 1)
                nc.vector.tensor_scalar(qst[:, g, :, :], qz[:, g * HG:(g + 1) * HG, bass.ds(b, 1), :].rearrange("p h o c -> p h (o c)"),
                                        1.0, None, ALU.mult).then_inc(q_staged, 1)

            def step(b, g):
                n = 2 * b + g
                new, combining, turning, _, (b2, g2) = stages(b, g)
                if new:
                    stage(b, g, isinstance(b, int) and b == 0)
                    for f in range(1, FILLS, 2):
                        dve.wait_ge(turned, FILLS * n + f + 1)
                        nc.vector.tensor_scalar(kt[:, f // 2, 512:1024], m.ps[:, f % 4, :], 1.0, None, ALU.mult).then_inc(kt_dve, 1)
                    dve.wait_ge(scored, n + 1)
                    wait(dve, exp_done, 2 * n)
                    nc.vector.tensor_tensor(sn[:, 0:NS], m.ps[:, 7, 0:NS], m.cst[:, C_MNEW:C_MNEW + NB * NS].rearrange("p (b t) -> p b t", b=NB)[
                        :, bass.ds(b, 1), :].rearrange("p o t -> p (o t)"), ALU.add).then_inc(masked, 1)
                    nc.vector.tensor_reduce(sn[:, NS:NS + 1], m.ps[:, 4:6, :].rearrange("p b k -> p (b k)"), AX.X, ALU.max).then_inc(max_two, 1)
                    dve.wait_ge(masked, n + 1)
                    dve.wait_ge(max_two, n + 1)
                    nc.vector.tensor_reduce(nmax[:, g:g + 1], sn[:, 0:NS + 1], AX.X, ALU.max, negate=True).then_inc(neg_max, 1)
                if combining:
                    dve.wait_ge(combined, n)
                    wait(dve, valued, n - 1)
                    nc.vector.tensor_scalar(pt[:, :, :], m.ps[:, 7, COMB:COMB + 16 * NPAGE].rearrange("p (n c) -> p n c", c=16), 1.0, None, ALU.mult).then_inc(pt_done, 1)
                    nc.vector.tensor_scalar(ptn[:, :], m.ps[0:NS, 7, COMB + 16 * NPAGE:COMB + 16 * NPAGE + 16], 1.0, None, ALU.mult).then_inc(pt_done, 1)
                if new:
                    dve.wait_ge(exp_done, 2 * n + 2)
                    nc.vector.tensor_tensor(sn[:, NS + 1:NS + 2], den[:, 0:1], den[:, 1:2], ALU.add).then_inc(den_done, 1)
                    dve.wait_ge(den_done, n + 1)
                    nc.vector.reciprocal(inv[:, 0:1], sn[:, NS + 1:NS + 2]).then_inc(inv_done, 1)
                    dve.wait_ge(inv_done, n + 1)
                    wait(dve, combined, n - 1)
                    nc.vector.tensor_scalar(cmb[:, g, :], m.comb[:, :], inv[:, 0:1], None, ALU.mult).then_inc(comb_done, 1)
                if turning:
                    dve.wait_ge(o_turned, n - 1)
                    nc.vector.tensor_scalar(o_s[:, g2 * HG:(g2 + 1) * HG, bass.ds(b2 * LS, LS)],
                                            m.ps[:, 7, TURN:TURN + 20 * HG].rearrange("p (h q) -> p h q", q=20)[:, :, 0:LS],
                                            1.0, None, ALU.mult).then_inc(o_done, 1)

            schedule(dve, step)
            dve.wait_ge(o_done, 2 * NB)
            of = o_s[:, :, :].rearrange("p h t -> p (h t)")
            nc.vector.tensor_tensor(o_q, of, of, ALU.mult).then_inc(sq_done, 1)
            dve.wait_ge(rs_done, 1)
            nc.vector.tensor_tensor(o_n, of, rs[:, 1, :], ALU.mult).then_inc(normed, 1)
            dve.wait_ge(normed, 1)
            nc.vector.tensor_scalar(of, o_n, m.gain[:, 6 * KT:6 * KT + 1], 1.0 - LAM_INIT, ALU.mult, ALU.mult).then_inc(gained, H)

        @block.tensor
        def _(pe):
            def keys(b, g):
                n = 2 * b + g
                pe.wait_ge(k_full[g], 16 * NPAGE * b + 16 * NPAGE)
                for f in range(FILLS):
                    if f % 2:
                        wait(pe, kt_dve, FILLS // 2 * n + (f - 5) // 2 + 1)
                    else:
                        wait(pe, kt_act, FILLS // 2 * n + (f - 4) // 2 + 1)
                    for t in range(4):
                        page = (f % 2) * 4 + t
                        mm = nc.tensor.transpose(m.ps[:, f % 4, t * P:(t + 1) * P], kb[:, g, page, (f // 2) * P:(f // 2 + 1) * P], ident)
                    mm.then_inc(turned, 1)

            def scores(b, g):
                n = 2 * b + g
                pe.wait_ge(q_staged, n + 1)
                pe.wait_ge(kt_act, FILLS // 2 * n + FILLS // 2)
                pe.wait_ge(kt_dve, FILLS // 2 * n + FILLS // 2)
                wait(pe, exp_done, 2 * n)
                for c in range(2):
                    for j in range(HG):
                        nc.tensor.matmul(m.ps[32 * j:32 * j + 32, 4 + c, :], qst[:, g, j, :], kt[:, j, c * 512:(c + 1) * 512], start=True, stop=True)
                wait(pe, o_done, n - 2)
                for j in range(HG):
                    mm = nc.tensor.matmul(m.ps[32 * j:32 * j + 32, 7, 0:NS], qst[:, g, j, :], m.k_s[:, g * HG + j, :], start=True, stop=True)
                mm.then_inc(scored, 1)

            def turn(n):
                pe.wait_ge(row_done, n - 1)
                pe.nop(nofuse=True)
                for j in range(HG):
                    mm = nc.tensor.transpose(m.ps[:, 7, TURN + 16 * j:TURN + 16 * j + 16], o_row[:, j * P:(j + 1) * P], ident[0:HG * LS, 0:HG * LS])
                mm.then_inc(o_turned, 1)

            def values(n, b1, g1):
                pe.wait_ge(comb_done, n)
                for t in range(NPAGE):
                    nc.tensor.matmul(m.ps[:, 7, COMB + 16 * t:COMB + 16 * t + 16], pr[:, g1, t * P:(t + 1) * P], cmb[:, g1, :], start=True, stop=True)
                nc.tensor.matmul(m.ps[0:NS, 7, COMB + 16 * NPAGE:COMB + 16 * NPAGE + 16], pr[:, g1, PAST:PAST + NS], cmb[:, g1, :],
                                 start=True, stop=True).then_inc(combined, 1)
                pe.wait_ge(pt_done, 2 * n)
                pe.wait_ge(v_full[g1], 16 * NPAGE * b1 + 16 * NPAGE)
                wait(pe, row_done, n - 1)
                for t in range(NPAGE):
                    nc.tensor.matmul(m.ps[0:HG * LS, 6, :], pt[:, t, :], vb[:, g1, t, :], start=(t == 0), stop=False)
                nc.tensor.matmul(m.ps[0:HG * LS, 6, :], ptn[:, :], m.v_s[0:NS, g1 * HG:(g1 + 1) * HG, :].rearrange("p h d -> p (h d)"),
                                 start=False, stop=True).then_inc(valued, 1)

            def step(b, g):
                n = 2 * b + g
                new, combining, turning, (b1, g1), _ = stages(b, g)
                if new:
                    keys(b, g)
                    scores(b, g)
                    pe.wait_ge(masked, n + 1)
                else:
                    pe.wait_ge(o_done, n - 2)
                if turning:
                    turn(n)
                if combining:
                    values(n, b1, g1)

            schedule(pe, step)
            pe.wait_ge(sq_done, 1)
            nc.tensor.matmul(m.ps[:, 0, 0:H * NS], m.cst[:, C_ONE:C_ONE + P], o_q, start=True, stop=True).then_inc(summed, 1)


NT = TT + 1
K_G, K_GC, K_EGC, K_EKD, K_BETA, K_BEGC, K_EGT, K_EGTS = range(8)
NCOL = 8


def delta_gates(nc, m, w_in):
    with ExitStack() as ctx:
        sem = semaphores(nc, ctx, "dg_")
        sb = lambda n, s, d=F32: ctx.enter_context(nc.sbuf_tensor("dg_" + n, s, d))
        raw_full, hi_done, lo_done, prod = (sem(n) for n in ("raw_full", "hi", "lo", "prod"))
        shifted, negabs, exp_neg, logged, soft, g_done, beta_done = (
            sem(n) for n in ("shifted", "negabs", "exp_neg", "logged", "soft", "g", "beta"))
        turned, moved, seq_done, summed, zeroed, part, exped, b_done = (
            sem(n) for n in ("turned", "moved", "seq", "summed", "zeroed", "part", "exped", "b"))
        raw = sb("raw", [P, KT, 16])
        hi = sb("hi", [P, KT, 16], F32R)
        lo = sb("lo", [P, KT, 16], F32R)
        x = sb("x", [H, T])
        na = sb("na", [H, T])
        lg = sb("lg", [H, T])
        g = sb("g", [H, T])
        beta = sb("beta", [H, T])
        gt = sb("gt", [P, NT, H])
        bt = sb("bt", [P, NT, H])
        gseq = sb("gseq", [NS, H, NB])
        tmp = sb("tmp", [P, NT, H])
        block = ctx.enter_context(nc.Block())
        ident = m.cst[:, C_ID:C_ID + P]

        def col(k):
            return m.cols[:, :, k, :].rearrange("p h t -> p t h")

        @block.sync
        def _(sp):
            sp.dma_start(raw[:, :, :], w_in.rearrange("o (f p) n -> p (o f) n", p=P)[:, :, OFF_AB:OFF_AB + 16]).then_inc(raw_full, 16)

        @block.scalar
        def _(act):
            act.wait_ge(raw_full, 16)
            nc.scalar.copy(hi[:, :, :], raw[:, :, :]).then_inc(hi_done, 1)
            act.wait_ge(negabs, 1)
            nc.scalar.activation(lg[:, :], na[:, :], ACT.Exp).then_inc(exp_neg, 1)
            act.wait_ge(exp_neg, 1)
            nc.scalar.activation(lg[:, :], lg[:, :], ACT.Ln, bias=m.cst[0:H, C_ONE:C_ONE + 1]).then_inc(logged, 1)
            act.wait_ge(prod, 6)
            nc.scalar.activation(beta[:, :].rearrange("p (c t) -> p c t", c=3), m.ps[0:H, 3:6, 0:CH], ACT.Sigmoid).then_inc(beta_done, 1)
            act.wait_ge(part, 3)
            nc.scalar.activation(col(K_EGC), col(K_GC), ACT.Exp).then_inc(exped, 1)
            act.wait_ge(part, 4)
            nc.scalar.activation(col(K_EKD), tmp[:, :, :], ACT.Exp).then_inc(exped, 1)
            nc.scalar.activation(m.cols[:, :, K_EGT, 0:TT].rearrange("p h t -> p t h"), m.ps[:, 1, 64:128].rearrange("p (t h) -> p t h", h=H), ACT.Exp).then_inc(exped, 1)
            nc.scalar.activation(m.cols[:, :, K_EGTS, 0:NB], m.ps[:, 1, 160:224].rearrange("p (h b) -> p h b", b=NB), ACT.Exp).then_inc(exped, 1)

        @block.vector
        def _(dve):
            nc.vector.memset(m.cols[:, :, :, :], 0.0).then_inc(zeroed, 1)
            nc.vector.memset(gt[:, :, :], 0.0).then_inc(zeroed, 1)
            nc.vector.memset(bt[:, :, :], 0.0).then_inc(zeroed, 1)
            nc.vector.memset(tmp[:, :, :], 0.0).then_inc(zeroed, 1)
            dve.wait_ge(hi_done, 1)
            nc.vector.tensor_tensor(lo[:, :, :], raw[:, :, :], hi[:, :, :].bitcast(F32), ALU.subtract).then_inc(lo_done, 1)
            dve.wait_ge(prod, 6)
            nc.vector.tensor_scalar(x[:, :].rearrange("p (c t) -> p c t", c=3), m.ps[0:H, 0:3, 0:CH], m.alog[0:H, 1:2], None, ALU.add).then_inc(shifted, 1)
            dve.wait_ge(shifted, 1)
            nc.vector.scalar_tensor_tensor(out=na[:, :], in0=x[:, :], scalar=-1.0, in1=x[:, :], op0=ALU.mult, op1=ALU.min).then_inc(negabs, 1)
            dve.wait_ge(logged, 1)
            nc.vector.scalar_tensor_tensor(out=na[:, :], in0=x[:, :], scalar=0.0, in1=lg[:, :], op0=ALU.max, op1=ALU.add).then_inc(soft, 1)
            dve.wait_ge(soft, 1)
            nc.vector.tensor_scalar(g[:, :], na[:, :], m.alog[0:H, 2:3], -1.0, ALU.mult, ALU.mult).then_inc(g_done, 1)
            dve.wait_ge(turned, 1)
            dve.wait_ge(zeroed, 4)
            for src, dst, o in ((0, gt, 0), (1, bt, 128)):
                v = m.ps[:, 6, o:o + NT * H].rearrange("p (t h) -> p t h", h=H)
                nc.vector.tensor_copy(dst[:, 0:TT, :], v[:, 0:TT, :]).then_inc(moved, 1)
                nc.vector.tensor_copy(dst[0:NS, TT, :], v[0:NS, TT, :]).then_inc(moved, 1)
            dve.wait_ge(moved, 4)
            nc.vector.tensor_tensor(gseq[:, :, :], gt[0:NS, TT, :].rearrange("p (h o) -> p h o", o=1).to_broadcast([NS, H, NB]),
                                    m.cst[0:NS, C_SEQ:C_SEQ + NB].rearrange("p (o b) -> p o b", o=1).to_broadcast([NS, H, NB]), ALU.mult).then_inc(seq_done, 1)
            nc.vector.tensor_copy(col(K_G), gt[:, :, :]).then_inc(b_done, 1)
            nc.vector.tensor_copy(col(K_BETA), bt[:, :, :]).then_inc(b_done, 1)
            dve.wait_ge(summed, 1)
            v = m.ps[:, 0, 0:NT * H].rearrange("p (t h) -> p t h", h=H)
            nc.vector.tensor_copy(col(K_GC)[:, 0:TT, :], v[:, 0:TT, :]).then_inc(part, 1)
            nc.vector.tensor_copy(col(K_GC)[0:NS, TT, :], v[0:NS, TT, :]).then_inc(part, 1)
            dve.wait_ge(part, 2)
            nc.vector.tensor_tensor(tmp[:, 0:TT, :], m.ps[:, 1, 64:128].rearrange("p (t h) -> p t h", h=H), col(K_GC)[:, 0:TT, :], ALU.subtract).then_inc(part, 1)
            nc.vector.tensor_tensor(tmp[0:NS, TT, :], m.ps[0:NS, 1, 128:136], col(K_GC)[0:NS, TT, :], ALU.subtract).then_inc(part, 1)
            dve.wait_ge(exped, 1)
            dve.wait_ge(b_done, 2)
            nc.vector.tensor_tensor(col(K_BEGC), col(K_BETA), col(K_EGC), ALU.mult).then_inc(b_done, 1)

        @block.tensor
        def _(pe):
            pe.wait_ge(lo_done, 1)
            for u in range(2):
                for c in range(3):
                    for f in range(KT):
                        for n, (a, b) in enumerate(((hi, m.p_hi), (hi, m.p_lo), (lo, m.p_hi))):
                            mm = nc.tensor.matmul(m.ps[0:H, 3 * u + c, 0:CH], a[:, f, u * H:(u + 1) * H], b[:, f, cols(c)],
                                                  start=(f == 0 and n == 0), stop=(f == KT - 1 and n == 2))
                    mm.then_inc(prod, 1)
            pe.wait_ge(g_done, 1)
            pe.wait_ge(beta_done, 1)
            for src, o in ((g, 0), (beta, 128)):
                for t in range(NT):
                    n = P if t < TT else NS
                    mm = nc.tensor.transpose(m.ps[0:n, 6, o + t * H:o + (t + 1) * H], src[:, t * P:t * P + n], ident[0:H, 0:H])
            mm.then_inc(turned, 1)
            pe.wait_ge(moved, 4)
            pe.wait_ge(seq_done, 1)
            flat = gt[:, 0:TT, :].rearrange("p t h -> p (t h)")
            nc.tensor.matmul(m.ps[:, 0, 0:TT * H], m.cst[:, C_TRI:C_TRI + P], flat, start=True, stop=True)
            nc.tensor.matmul(m.ps[0:NS, 0, TT * H:NT * H], m.cst[0:NS, C_TRI4:C_TRI4 + NS], gt[0:NS, TT, :], start=True, stop=True)
            nc.tensor.matmul(m.ps[:, 1, 64:128], m.cst[:, C_ONE:C_ONE + P], flat, start=True, stop=True)
            nc.tensor.matmul(m.ps[0:NS, 1, 128:136], m.cst[0:NS, C_SAME:C_SAME + NS], gt[0:NS, TT, :], start=True, stop=True)
            nc.tensor.matmul(m.ps[:, 1, 160:224], m.cst[0:NS, C_ONE:C_ONE + P], gseq[:, :, :].rearrange("p h b -> p (h b)"),
                             start=True, stop=True).then_inc(summed, 1)


def delta_heads(nc, m, w_in, o_dram, state, conv_prompt, conv_sample, delta_prompt, delta_sample):
    with ExitStack() as ctx:
        sem = semaphores(nc, ctx, "dl_")
        sb = lambda n, s, d=F32: ctx.enter_context(nc.sbuf_tensor("dl_" + n, s, d))
        raw_full = [sem("raw_full0"), sem("raw_full1")]
        hi_done, lo_done, proj_mm, taken = (sem(n) for n in ("w_hi", "w_lo", "proj_mm", "taken"))
        padded, conv_done, silu_done, tail_done, tail_mm, tail_moved, tail_out = (
            sem(n) for n in ("padded", "conv", "silu", "tail", "tail_mm", "tail_moved", "tail_out"))
        tok_mm, tok_moved, squared, sum_sq, ln_done, rs_done, rs_q, normed = (
            sem(n) for n in ("tok_mm", "tok_moved", "squared", "sum_sq", "ln", "rs", "rs_q", "normed"))
        staged, qd_done, kp_done, kd_done, vb_done, km_done, bt_mm, bt_moved = (
            sem(n) for n in ("staged", "qd", "kp", "kd", "vb", "km", "bt_mm", "bt_moved"))
        gc_mm, diff_done, clamp_done, decay_done, tri_done, gq_mm, low_done, qk_done = (
            sem(n) for n in ("gc_mm", "diff", "clamp", "decay", "tri", "gq_mm", "low", "qk"))
        mask_done, p_mm, p_moved, t_mm, t_moved, r_mm, u_done, w_mm, w_moved = (
            sem(n) for n in ("mask", "p_mm", "p_moved", "t_mm", "t_moved", "r_mm", "u", "w_mm", "w_moved"))
        v_mm, v_moved, o_mm, o_moved, s_mm, s_done, state_in, state_out = (
            sem(n) for n in ("v_mm", "v_moved", "o_mm", "o_moved", "s_mm", "s", "state_in", "state_out"))
        o_sq, o_sq_s, o_sum, o_ln, o_rs, o_normed, d_mm, z_done, out_done, s_decayed, pad_zero = (
            sem(n) for n in ("o_sq", "o_sq_s", "o_sum", "o_ln", "o_rs", "o_normed", "d_mm", "z", "out", "s_decayed", "pad_zero"))
        LAST = LEVELS - 1
        SX = CW - 1 + LP
        XC = SX + NB * (CW - 1 + LS)
        CO = XC - (CW - 1)
        xc = sb("xc", [P, 3, XC])
        cs = sb("cs", [P, 3, XC])
        css = sb("css", [P, 3, NS])
        zs = sb("zs", [P, T])
        tail = sb("tail", [P, 27 * 3])
        tails = sb("tails", [27, 3, P])
        tok = sb("tok", [P, NT, 3, P])
        ssq = sb("ssq", [P, 4, NT, 2])
        col = sb("col", [P, NCOL, NT])
        kp = sb("kp", [P, NT, P])
        kd = sb("kd", [P, NT, P])
        orow = sb("orow", [P, NT, P])
        bt = sb("bt", [P, NT, 3, P])
        lo_t = sb("lo_t", [P, NT, P])
        qk_t = sb("qk_t", [P, NT, P])
        mk = sb("mk", [P, 2, 4, P])
        uu = sb("uu", [P, NT, P])
        tt = sb("tt", [P, 2, 4, P])
        pp = sb("pp", [P, 2, 4, P])
        dif = pp[:, 0, :, :]
        km = tt[0:NS, :, :, :].rearrange("p a b d -> p (a b) d")
        vn = sb("vn", [P, 2, P])
        vnt = sb("vnt", [P, 2, NS])
        wq = sb("wq", [P, NB, 2, LS])
        st = sb("st", [P, P])
        sts = sb("sts", [P, NB, P])
        block = ctx.enter_context(nc.Block())
        win = w_in.rearrange("o (f p) n -> p (o f) n", p=P)
        ident = m.cst[:, C_ID:C_ID + P]
        tri = m.cst[:, C_TRI:C_TRI + P]

        def by_sequence(k):
            return m.ps[:, 2, 0:2 * NS].rearrange("p (b k l) -> p b k l", k=2, l=LS)[:, :, k, :]

        def sample_cols(a):
            return a[:, SX:SX + NB * 7].rearrange("p (b w) -> p b w", w=7)

        def unit_src(h, u):
            return win[:, :, bass.ds(OFF_QKVB + u * D + h * P, P)] if u < 3 else win[:, :, bass.ds(OFF_Z + h * P, P)]

        def schedule(eng, first, head):
            first()
            head(0, True)
            with eng.Fori(1, H - 1) as h:
                head(h, True)
            head(H - 1, False)

        def tile(t):
            return (P, slice(t * P, (t + 1) * P)) if t < TT else (NS, slice(0, NS))

        @block.sync
        def _(sp):
            def load(n, k, src):
                wait(sp, lo_done, n - 1)
                sp.dma_start(m.w_raw[:, k, :].rearrange("p (f n) -> p f n", n=P), src).then_inc(raw_full[k], 16)

            def first():
                for u in range(3):
                    load(u, u % 2, unit_src(0, u))

            def head(h, more):
                load(4 * h + 3, 1, unit_src(h, 3))
                if more:
                    load(4 * h + 4, 0, unit_src(h + 1, 0))
                wait(sp, state_out, 32 * h)
                sp.dma_start(sts[:, :, :], state.rearrange("o b h k v -> k (o b) h v")[:, :, bass.ds(h, 1), :].rearrange("k b o v -> k b (o v)")).then_inc(state_in, 16)
                if more:
                    for u in range(1, 3):
                        load(4 * h + 4 + u, u % 2, unit_src(h + 1, u))

            schedule(sp, first, head)

        @block.scalar
        def _(act):
            def high(n, k):
                act.wait_ge(raw_full[k], 8 * (n - k) + 16)
                nc.scalar.copy(m.w_hi[:, k, :], m.w_raw[:, k, :]).then_inc(hi_done, 1)

            def take(h, u, c, n):
                g = 3 * n + c
                bank = (u + c) % 2
                act.wait_ge(proj_mm, g + 1)
                if c == 0:
                    wait(act, conv_done, 12 * (h - 1) + 4 * u + 4)
                    wait(act, tail_done, 6 * h)
                if c < 2:
                    nc.scalar.copy(xc[:, u, 3 + c * CH:3 + (c + 1) * CH], m.ps[:, bank, 0:CH]).then_inc(taken, 1)
                else:
                    nc.scalar.copy(xc[:, u, 3 + 2 * CH:3 + LP], m.ps[:, bank, 0:LP - 2 * CH])
                    nc.scalar.copy(sample_cols(xc[:, u, :])[:, :, 3:7],
                                   m.ps[:, bank, LP - 2 * CH:CH].rearrange("p (b l) -> p b l", l=LS)).then_inc(taken, 1)
                    if u < 2:
                        high(n + 2, u % 2)

            def silus(h, u):
                act.wait_ge(conv_done, 12 * h + 4 * u + 4)
                nc.scalar.activation(cs[:, u, 0:LP], cs[:, u, 0:LP], ACT.Silu)
                nc.scalar.activation(css[:, u, :].rearrange("p (b l) -> p b l", l=LS), sample_cols(cs[:, u, :])[:, :, 0:LS], ACT.Silu).then_inc(silu_done, 1)

            def first():
                high(0, 0)
                high(1, 1)
                for u in range(3):
                    for c in range(3):
                        take(0, u, c, u)
                for u in range(3):
                    silus(0, u)

            def head(h, more):
                def gate(c):
                    act.wait_ge(proj_mm, 12 * h + 9 + c + 1)
                    if c == 0:
                        wait(act, out_done, 16 * h)
                    nc.scalar.activation(zs[:, cols(c)], m.ps[:, (3 + c) % 2, 0:CH], ACT.Silu).then_inc(taken, 1)

                if more:
                    high(4 * h + 4, 0)
                for t in range(NT):
                    n, _ = tile(t)
                    act.wait_ge(tok_mm, NT * h + t + 1)
                    if t == 0:
                        wait(act, s_done, (TT + 2) * h)
                        act.wait_ge(pad_zero, 2)
                    nc.scalar.copy(tok[0:n, t, :, :], m.ps[0:n, 2 + t % 2, 0:3 * P].rearrange("p (k d) -> p k d", d=P)).then_inc(tok_moved, 1)
                act.wait_ge(tok_moved, NT * h + NT)
                sq = bt[:, :, 0:2, :]
                nc.scalar.activation(sq, tok[:, :, 0:2, :], ACT.Square).then_inc(squared, 1)
                gate(0)
                act.wait_ge(sum_sq, h + 1)
                nc.scalar.activation(ssq[:, 1, :, :], ssq[:, 0, :, :], ACT.Ln, bias=m.cst[:, C_EPS:C_EPS + 1]).then_inc(ln_done, 1)
                act.wait_ge(ln_done, h + 1)
                nc.scalar.activation(ssq[:, 2, :, :], ssq[:, 1, :, :], ACT.Exp, scale=-0.5).then_inc(rs_done, 1)
                act.wait_ge(tail_mm, h + 1)
                wait(act, tail_out, 32 * h)
                nc.scalar.copy(tails[:, :, :], m.ps[0:27, 6, 0:3 * P].rearrange("p (k d) -> p k d", d=P)).then_inc(tail_moved, 1)
                gate(1)
                gate(2)
                for t in range(NT):
                    n, _ = tile(t)
                    act.wait_ge(bt_mm, NT * h + t + 1)
                    ins = nc.scalar.copy(bt[:, t, :, 0:n], m.ps[:, 4 + t % 2, 0:3 * P].rearrange("p (k d) -> p k d", d=P)[:, :, 0:n])
                    if t < TT:
                        ins.then_inc(bt_moved, 1)
                    else:
                        nc.scalar.copy(wq[:, :, 1, :], m.ps[:, 4 + t % 2, 2 * P:2 * P + NS].rearrange("p (b l) -> p b l", l=LS)).then_inc(bt_moved, 1)
                for x in range(3):
                    k, n = (4, P) if x < 2 else (1, NS)
                    act.wait_ge(clamp_done, 6 * h + 2 * x + 2)
                    nc.scalar.activation(lo_t[0:n, 4 * x:4 * x + k, 0:n], lo_t[0:n, 4 * x:4 * x + k, 0:n], ACT.Exp, scale=-1.0).then_inc(decay_done, 1)
                    nc.scalar.activation(qk_t[0:n, 4 * x:4 * x + k, 0:n], qk_t[0:n, 4 * x:4 * x + k, 0:n], ACT.Exp).then_inc(decay_done, 1)
                if more:
                    high(4 * h + 5, 1)
                    for c in range(3):
                        take(h + 1, 0, c, 4 * h + 4)

                def moves(i, x, k, n):
                    b = x % 2
                    act.wait_ge(p_mm, 16 * h + i[0] + 1)
                    nc.scalar.copy(pp[0:n, b, 0:k, 0:n], m.ps[0:n, 4 + b, :].rearrange("p (k d) -> p k d", d=P)[:, 0:k, 0:n]).then_inc(p_moved, 1)
                    act.wait_ge(t_mm, 13 * h + i[1] + 1)
                    nc.scalar.copy(tt[0:n, b, 0:k, 0:n], m.ps[0:n, 2 + b, :].rearrange("p (k d) -> p k d", d=P)[:, 0:k, 0:n]).then_inc(t_moved, 1)

                for lev in range(1, LEVELS):
                    for x in range(2):
                        moves((2 * lev + x, 2 * (lev - 1) + x), x, 4, P if lev < LAST else P // 2)
                moves((15, 12), 2, 1, NS)
                for x in range(3):
                    k, n = (4, P) if x < 2 else (1, NS)
                    act.wait_ge(w_mm, 3 * h + x + 1)
                    if x < 2:
                        nc.scalar.mul(kp[:, 4 * x:4 * x + 4, :], m.ps[:, 6 + x, :].rearrange("p (k d) -> p k d", d=P), -1.0).then_inc(w_moved, 1)
                    else:
                        nc.scalar.mul(wq[:, :, 0, :], m.ps[:, 6, 0:NS].rearrange("p (b l) -> p b l", l=LS), -1.0).then_inc(w_moved, 1)
                for t in range(TT):
                    act.wait_ge(v_mm, (TT + 2) * h + t + 1)
                    nc.scalar.copy(vn[:, t % 2, :], m.ps[:, 2 + t % 2, 0:P]).then_inc(v_moved, 1)
                    act.wait_ge(o_mm, (TT + 2) * h + t + 1)
                    nc.scalar.copy(orow[:, t, :], m.ps[:, 4 + t % 2, 0:P]).then_inc(o_moved, 1)
                    if more and t < 6:
                        take(h + 1, 1 + t // 3, t % 3, 4 * h + 5 + t // 3)
                    if more and t in (3, 6):
                        silus(h + 1, t // 3 - 1)
                act.wait_ge(o_moved, (TT + 2) * h + TT)
                nc.scalar.activation(bt[:, 0:TT, 0, :], orow[:, 0:TT, :], ACT.Square).then_inc(o_sq, 1)
                act.wait_ge(v_mm, (TT + 2) * h + TT + 1)
                nc.scalar.copy(vnt[:, 0, :].rearrange("p (b l) -> p b l", l=LS), by_sequence(0)).then_inc(v_moved, 1)
                act.wait_ge(v_mm, (TT + 2) * h + TT + 2)
                nc.scalar.copy(vn[0:NS, 0, :], m.ps[0:NS, 3, 0:P]).then_inc(v_moved, 1)
                act.wait_ge(o_mm, (TT + 2) * h + TT + 1)
                nc.scalar.copy(vnt[:, 1, :].rearrange("p (b l) -> p b l", l=LS), by_sequence(1)).then_inc(o_moved, 1)
                act.wait_ge(o_mm, (TT + 2) * h + TT + 2)
                nc.scalar.copy(orow[0:NS, TT, :], m.ps[0:NS, 5, 0:P]).then_inc(o_moved, 1)
                act.wait_ge(o_moved, (TT + 2) * (h + 1))
                nc.scalar.activation(bt[:, TT, 0, :], orow[:, TT, :], ACT.Square, accum_out=ssq[:, 3, TT, 0:1]).then_inc(o_sq_s, 1)
                act.wait_ge(o_sq_s, h + 1)
                act.wait_ge(o_sum, h + 1)
                nc.scalar.activation(ssq[:, 1, :, 0], ssq[:, 3, :, 0], ACT.Ln, scale=1.0 / P, bias=m.cst[:, C_EPS:C_EPS + 1]).then_inc(o_ln, 1)
                act.wait_ge(o_ln, h + 1)
                nc.scalar.activation(ssq[:, 3, :, 1], ssq[:, 1, :, 0], ACT.Exp, scale=-0.5).then_inc(o_rs, 1)
                if more:
                    silus(h + 1, 2)

            schedule(act, first, head)

        @block.vector
        def _(dve):
            def low(n, k):
                dve.wait_ge(hi_done, n + 1)
                nc.vector.tensor_tensor(m.w_lo[:, k, :], m.w_raw[:, k, :], m.w_hi[:, k, :].bitcast(F32), ALU.subtract).then_inc(lo_done, 1)

            def conv(h, u, n):
                dve.wait_ge(taken, 3 * n + 3)
                wait(dve, tok_mm, NT * h)
                wgt = m.convw[:, bass.ds(h + u * H, 1), :].rearrange("p o w -> p (o w)")
                nc.vector.tensor_scalar(sample_cols(xc[:, u, :])[:, :, 0:3], m.cst8[:, bass.ds(h + u * H, 1), :].rearrange("p o (b w) -> p (o b) w", w=3),
                                        1.0, None, ALU.mult).then_inc(padded, 1)
                dve.wait_ge(padded, 3 * h + u + 2)
                nc.vector.tensor_scalar(cs[:, u, 0:CO], xc[:, u, 0:CO], wgt[:, 0:1], None, ALU.mult).then_inc(conv_done, 1)
                product(h, u, 1)

            def product(h, u, i):
                wgt = m.convw[:, bass.ds(h + u * H, 1), :].rearrange("p o w -> p (o w)")
                dve.wait_ge(conv_done, 12 * h + 4 * u + i)
                nc.vector.scalar_tensor_tensor(out=cs[:, u, 0:CO], in0=xc[:, u, i:i + CO], scalar=wgt[:, i:i + 1], in1=cs[:, u, 0:CO],
                                               op0=ALU.mult, op1=ALU.add).then_inc(conv_done, 1)

            def conv_rest(h, u):
                product(h, u, 2)
                product(h, u, 3)
                if u == 0:
                    wait(dve, tail_mm, h)
                nc.vector.tensor_copy(tail[:, 27 * u:27 * u + 3], xc[:, u, LP:LP + 3]).then_inc(tail_done, 1)
                nc.vector.tensor_copy(tail[:, 27 * u + 3:27 * u + 27].rearrange("p (b w) -> p b w", w=3), sample_cols(xc[:, u, :])[:, :, 4:7]).then_inc(tail_done, 1)

            def first():
                nc.vector.memset(xc[:, :, 0:CW - 1], 0.0).then_inc(padded, 1)
                nc.vector.memset(orow[:, TT, :], 0.0).then_inc(pad_zero, 1)
                nc.vector.memset(tok[:, TT, :, :], 0.0).then_inc(pad_zero, 1)
                low(0, 0)
                low(1, 1)
                for u in range(3):
                    if u < 2:
                        low(u + 2, u)
                    conv(0, u, u)
                    conv_rest(0, u)

            def head(h, more):
                if more:
                    low(4 * h + 4, 0)
                dve.wait_ge(squared, h + 1)
                nc.vector.tensor_reduce(ssq[:, 0, :, :], bt[:, :, 0:2, :], AX.X, ALU.add).then_inc(sum_sq, 1)
                wait(dve, s_done, (TT + 2) * h)
                nc.vector.tensor_scalar(col[:, :, :], m.cols[:, bass.ds(h, 1), :, :].rearrange("p o k t -> p (o k) t"), 1.0, None, ALU.mult).then_inc(staged, 1)
                dve.wait_ge(rs_done, h + 1)
                nc.vector.tensor_scalar(ssq[:, 2, :, 0], ssq[:, 2, :, 0], float(P) ** -0.5, None, ALU.mult).then_inc(rs_q, 1)
                dve.wait_ge(rs_q, h + 1)
                qk = tok[:, :, 0:2, :]
                nc.vector.tensor_tensor(qk, qk, ssq[:, 2, :, :].rearrange("p t (k o) -> p t k o", o=1).to_broadcast([P, NT, 2, P]), ALU.mult).then_inc(normed, 1)
                dve.wait_ge(normed, h + 1)
                dve.wait_ge(staged, h + 1)
                wait(dve, o_normed, h)
                wait(dve, d_mm, 3 * h)
                nc.vector.tensor_tensor(orow[:, :, :], tok[:, :, 0, :], by_token(K_EGC), ALU.mult).then_inc(qd_done, 1)
                for x in range(3):
                    k, n = (4, P) if x < 2 else (1, NS)
                    a, b = 4 * x, 4 * x + k
                    dve.wait_ge(gc_mm, 3 * h + x + 1)
                    wait(dve, clamp_done, 6 * h + 2 * x)
                    nc.vector.tensor_tensor(dif[0:n, 0:k, 0:n], m.ps[0:n, 6 + x % 2, :].rearrange("p (k d) -> p k d", d=P)[:, 0:k, 0:n],
                                            by_token(K_GC)[0:n, a:b, 0:n], ALU.subtract).then_inc(diff_done, 1)
                    dve.wait_ge(diff_done, 3 * h + x + 1)
                    nc.vector.tensor_scalar(lo_t[0:n, a:b, 0:n], dif[0:n, 0:k, 0:n], 0.0, None, ALU.max).then_inc(clamp_done, 1)
                    nc.vector.tensor_scalar(qk_t[0:n, a:b, 0:n], dif[0:n, 0:k, 0:n], 0.0, None, ALU.min).then_inc(clamp_done, 1)
                for t in range(NT):
                    n, _ = tile(t)
                    v = m.ps[0:n, 2 + (t // 2) % 2, (t % 2) * 256:(t % 2) * 256 + 256].rearrange("p (k d) -> p k d", d=P)
                    dve.wait_ge(gq_mm, 5 * h + t // 2 + 1)
                    dve.wait_ge(decay_done, 6 * h + 2 * (t // 4) + 2)
                    dve.wait_ge(tri_done, 3 * h + t // 4 + 1)
                    nc.vector.scalar_tensor_tensor(out=lo_t[0:n, t, 0:n], in0=v[:, 0, 0:n], scalar=col[0:n, K_BETA, t:t + 1], in1=lo_t[0:n, t, 0:n],
                                                   op0=ALU.mult, op1=ALU.mult).then_inc(low_done, 1)
                    nc.vector.tensor_tensor(qk_t[0:n, t, 0:n], v[:, 1, 0:n], qk_t[0:n, t, 0:n], ALU.mult).then_inc(qk_done, 1)

                def update(i, x, k, n, level0, j):
                    b = x % 2
                    u = uu[0:n, 4 * x:4 * x + k, 0:n]
                    if level0:
                        dve.wait_ge(p_mm, 16 * h + i + 1)
                        nc.vector.tensor_tensor(u, ident[0:n, 0:n].rearrange("p (o d) -> p o d", o=1).to_broadcast([n, k, n]),
                                                m.ps[0:n, 4 + b, :].rearrange("p (k d) -> p k d", d=P)[:, 0:k, 0:n], ALU.subtract).then_inc(u_done, 1)
                    else:
                        dve.wait_ge(r_mm, 13 * h + i + 1)
                        dve.wait_ge(u_done, 16 * h + j)
                        if n == P // 2:
                            u = uu[0:n, 4 * x:4 * x + k, n:P]
                        nc.vector.tensor_tensor(u, u, m.ps[0:n, 6 + b, :].rearrange("p (k d) -> p k d", d=P)[:, 0:k, 0:n], ALU.subtract).then_inc(u_done, 1)

                for x in range(2):
                    update(x, x, 4, P, True, 0)
                if more:
                    low(4 * h + 5, 1)
                for lev in range(1, LEVELS):
                    for x in range(2):
                        update(2 * (lev - 1) + x, x, 4, P if lev < LAST else P // 2, False, 2 * lev + x - 1)
                update(14, 2, 1, NS, True, 0)
                update(12, 2, 1, NS, False, 15)
                if more:
                    low(4 * h + 6, 0)
                for t in range(TT):
                    if t == 0:
                        dve.wait_ge(s_mm, (TT + 2) * h + 1)
                        wait(dve, state_out, 32 * h)
                        nc.vector.tensor_copy(st[:, :], m.ps[:, 6, 0:P]).then_inc(s_done, 1)
                    else:
                        dve.wait_ge(s_mm, (TT + 2) * h + t + 1)
                        dve.wait_ge(s_done, (TT + 2) * h + t)
                        dve.wait_ge(o_mm, (TT + 2) * h + t + 1)
                        nc.vector.scalar_tensor_tensor(out=st[:, :], in0=st[:, :], scalar=col[:, K_EGT, t:t + 1], in1=m.ps[:, 6 + t % 2, 0:P],
                                                       op0=ALU.mult, op1=ALU.add).then_inc(s_done, 1)
                    if more and t in (0, 3, 6):
                        conv(h + 1, t // 3, 4 * h + 4 + t // 3)
                    if more and t in (1, 4, 7):
                        conv_rest(h + 1, t // 3)
                    if more and t == 2:
                        low(4 * h + 7, 1)
                dve.wait_ge(o_sq, h + 1)
                nc.vector.tensor_reduce(ssq[:, 3, 0:TT, 0], bt[:, 0:TT, 0, :], AX.X, ALU.add).then_inc(o_sum, 1)
                dve.wait_ge(v_mm, (TT + 2) * h + TT + 1)
                dve.wait_ge(state_in, 16 * h + 16)
                nc.vector.tensor_tensor(sts[:, :, :], sts[:, :, :], col[:, K_EGTS, 0:NB].rearrange("p (b o) -> p b o", o=1).to_broadcast([P, NB, P]),
                                        ALU.mult).then_inc(s_decayed, 1)
                dve.wait_ge(s_decayed, h + 1)
                for g in range(2):
                    dve.wait_ge(s_mm, (TT + 2) * h + TT + g + 1)
                    nc.vector.tensor_tensor(sts[:, 4 * g:4 * g + 4, :], sts[:, 4 * g:4 * g + 4, :],
                                            m.ps[:, 6 + g, :].rearrange("p (b v) -> p b v", v=P), ALU.add).then_inc(s_done, 1)
                dve.wait_ge(o_rs, h + 1)
                nc.vector.tensor_tensor(orow[:, :, :], orow[:, :, :], ssq[:, 3, :, 1:2].to_broadcast([P, NT, P]), ALU.mult).then_inc(o_normed, 1)
                for g in range(3):
                    a, b = (512 * g, 512 * g + 512) if g < 2 else (LP, T)
                    dve.wait_ge(d_mm, 3 * h + g + 1)
                    if g == 0:
                        dve.wait_ge(taken, 12 * h + 12)
                    nc.vector.scalar_tensor_tensor(out=zs[:, a:b], in0=m.ps[:, 2 + g, 0:b - a], scalar=m.gain[:, 6 * KT + 1:6 * KT + 2], in1=zs[:, a:b],
                                                   op0=ALU.mult, op1=ALU.mult).then_inc(z_done, 1)

            def by_token(k):
                return col[:, k, :].rearrange("p (t o) -> p t o", o=1).to_broadcast([P, NT, P])

            schedule(dve, first, head)

        @block.gpsimd
        def _(pool):
            def by_token(k):
                return col[:, k, :].rearrange("p (t o) -> p t o", o=1).to_broadcast([P, NT, P])

            def first():
                pass

            def head(h, more):
                pool.wait_ge(normed, h + 1)
                pool.wait_ge(staged, h + 1)
                wait(pool, s_mm, (TT + 2) * h)
                wait(pool, v_mm, (TT + 2) * h)
                nc.gpsimd.tensor_tensor(kp[:, :, :], tok[:, :, 1, :], by_token(K_BEGC), ALU.mult).then_inc(kp_done, 1)
                pool.wait_ge(decay_done, 6 * h + 2)
                nc.gpsimd.tensor_tensor(qk_t[:, 0:4, :], qk_t[:, 0:4, :], tri.rearrange("p (o d) -> p o d", o=1).to_broadcast([P, 4, P]), ALU.mult).then_inc(tri_done, 1)
                pool.wait_ge(decay_done, 6 * h + 4)
                nc.gpsimd.tensor_tensor(qk_t[:, 4:8, :], qk_t[:, 4:8, :], tri.rearrange("p (o d) -> p o d", o=1).to_broadcast([P, 4, P]), ALU.mult).then_inc(tri_done, 1)
                pool.wait_ge(decay_done, 6 * h + 6)
                nc.gpsimd.tensor_tensor(qk_t[0:NS, TT, 0:NS], qk_t[0:NS, TT, 0:NS], m.cst[0:NS, C_TRI4:C_TRI4 + NS], ALU.mult).then_inc(tri_done, 1)

                def mask(lev, x, k, n, j):
                    msk = m.cst[0:n, C_LEV + lev * P:C_LEV + lev * P + n].rearrange("p (o d) -> p o d", o=1).to_broadcast([n, k, n])
                    wait(pool, p_mm, j)
                    nc.gpsimd.tensor_tensor(mk[0:n, x % 2, 0:k, 0:n], lo_t[0:n, 4 * x:4 * x + k, 0:n], msk, ALU.mult).then_inc(mask_done, 1)

                for lev in range(LEVELS):
                    for x in range(2):
                        if lev == 0:
                            pool.wait_ge(low_done, NT * h + 4 * x + 4)
                        mask(lev, x, 4, P, 16 * h + (2 * lev + x - 1 if lev else 0))
                    if lev == 0:
                        nc.gpsimd.tensor_tensor(kd[:, :, :], tok[:, :, 1, :], by_token(K_EKD), ALU.mult).then_inc(kd_done, 1)
                    if lev == 1:
                        v = tok[:, :, 2, :]
                        nc.gpsimd.tensor_tensor(v, v, by_token(K_BETA), ALU.mult).then_inc(vb_done, 1)
                pool.wait_ge(low_done, NT * h + NT)
                mask(0, 2, 1, NS, 16 * h + 13)
                mask(1, 2, 1, NS, 16 * h + 15)
                pool.wait_ge(kd_done, h + 1)
                pool.wait_ge(r_mm, 13 * h + 13)
                nc.gpsimd.tensor_tensor(km[:, :, :], kd[0:NS, TT:TT + 1, :].to_broadcast([NS, NB, P]),
                                                m.cst[0:NS, C_SEQ:C_SEQ + NB].rearrange("p (b o) -> p b o", o=1).to_broadcast([NS, NB, P]), ALU.mult).then_inc(km_done, 1)
                pool.wait_ge(tail_moved, h + 1)
                for n, (dst, a, b) in enumerate(((conv_prompt, 0, 3), (conv_sample, 3, 27))):
                    rows = dst.rearrange("o b w (k h d) -> (o b w) k h d", k=3, d=P)
                    pool.dma_start(rows[:, :, bass.ds(h, 1), :].rearrange("r k o d -> r k (o d)"), tails[a:b, :, :]).then_inc(tail_out, 16)
                pool.wait_ge(z_done, 3 * h + 3)
                pool.dma_start(o_dram[bass.ds(h, 1)].rearrange("o p t -> (o p) t"), zs[:, :]).then_inc(out_done, 16)
                pool.wait_ge(s_done, (TT + 2) * (h + 1))
                pool.dma_start(delta_prompt.rearrange("o b h k v -> (o b h) k v")[bass.ds(h, 1)].rearrange("o k v -> (o k) v"), st[:, :]).then_inc(state_out, 16)
                pool.dma_start(delta_sample.rearrange("o b h k v -> k (o b) h v")[:, :, bass.ds(h, 1), :].rearrange("k b o v -> k b (o v)"), sts[:, :, :]).then_inc(state_out, 16)

            schedule(pool, first, head)
            pool.wait_ge(tail_out, 32 * H)
            pool.wait_ge(out_done, 16 * H)
            pool.wait_ge(state_out, 32 * H)

        @block.tensor
        def _(pe):
            def wait_small(*waits):
                for s, v in waits:
                    pe.wait_ge(s, v)
                pe.nop(nofuse=True)

            def group(u, c, n):
                if c == 0:
                    pe.wait_ge(lo_done, n + 1)
                wait(pe, taken, 3 * n + c - 1)
                for f in range(KT):
                    w = slice(f * P, (f + 1) * P)
                    for i, (a, x) in enumerate(((m.w_hi, m.p_hi), (m.w_hi, m.p_lo), (m.w_lo, m.p_hi))):
                        mm = nc.tensor.matmul(m.ps[:, (u + c) % 2, 0:CH], a[:, u % 2, w], x[:, f, cols(c)],
                                              start=(f == 0 and i == 0), stop=(f == KT - 1 and i == 2))
                mm.then_inc(proj_mm, 1)

            def first():
                for u in range(3):
                    for c in range(3):
                        group(u, c, u)
                group(3, 0, 3)

            def head(h, more):
                S = (TT + 2) * h
                pe.wait_ge(silu_done, 3 * h + 3)
                for t in range(NT):
                    n, r = tile(t)
                    if t < 2:
                        wait(pe, z_done, 3 * h)
                    else:
                        pe.wait_ge(tok_moved, NT * h + t - 1)
                    for u in range(3):
                        src = cs[:, u, t * P:(t + 1) * P] if t < TT else css[:, u, :]
                        mm = nc.tensor.transpose(m.ps[0:n, 2 + t % 2, u * P:(u + 1) * P], src, ident)
                    mm.then_inc(tok_mm, 1)
                pe.wait_ge(tail_done, 6 * h + 6)
                wait(pe, s_done, S)
                for u in range(3):
                    mm = nc.tensor.transpose(m.ps[0:27, 6, u * P:(u + 1) * P], tail[:, 27 * u:27 * u + 27], ident)
                mm.then_inc(tail_mm, 1)
                group(3, 1, 4 * h + 3)
                group(3, 2, 4 * h + 3)
                if more:
                    group(0, 0, 4 * h + 4)
                pe.wait_ge(qd_done, h + 1)
                for t in range(NT):
                    n, r = tile(t)
                    if t < 2:
                        wait(pe, z_done, 3 * h)
                        wait(pe, o_moved, S)
                    elif t < TT:
                        pe.wait_ge(bt_moved, NT * h + t - 1)
                    else:
                        wait_small((bt_moved, NT * h + t - 1))
                    for i, src in enumerate((tok[0:n, t, 1, :], tok[0:n, t, 0, :], orow[0:n, t, :])):
                        mm = nc.tensor.transpose(m.ps[:, 4 + t % 2, i * P:i * P + n], src, ident[0:n, 0:n])
                    mm.then_inc(bt_mm, 1)
                for x in range(3):
                    k, n = (4, P) if x < 2 else (1, NS)
                    if x == 0:
                        pe.wait_ge(tail_moved, h + 1)
                    if x == 2:
                        wait_small((diff_done, 3 * h + 1))
                    for j in range(k):
                        t = 4 * x + j
                        mm = nc.tensor.matmul(m.ps[0:n, 6 + x % 2, j * P:j * P + n], col[0:n, K_G, t:t + 1].to_broadcast([n, n]),
                                              (tri if x < 2 else m.cst[0:NS, C_TRI4:C_TRI4 + NS]), start=True, stop=True)
                    mm.then_inc(gc_mm, 1)
                for t in range(NT):
                    n, r = tile(t)
                    if more and t == 4:
                        group(0, 1, 4 * h + 4)
                    if t % 2 == 0:
                        pe.wait_ge(bt_moved, NT * h + min(t + 2, NT))
                        pe.wait_ge(tok_moved, NT * h + NT)
                        if t >= 4:
                            pe.wait_ge(qk_done, NT * h + t - 2)
                    out = m.ps[0:n, 2 + (t // 2) % 2, (t % 2) * 256:(t % 2) * 256 + 256].rearrange("p (i d) -> p i d", i=2)
                    mm = nc.tensor.matmul(out[:, :, 0:n], bt[:, t, 0, 0:n], bt[:, t, 0:2, 0:n], start=True, stop=True)
                    if t % 2 == 1 or t == TT:
                        mm.then_inc(gq_mm, 1)

                def pmul(i, x, k, n, rhs):
                    if n >= P // 2:
                        pe.wait_ge(mask_done, 16 * h + i + 1)
                    if n == P // 2:
                        pe.nop(nofuse=True)
                    for j in range(k):
                        if n == P // 2:
                            mm = nc.tensor.matmul(m.ps[0:n, 4 + x % 2, j * P:j * P + n], mk[n:P, x % 2, j, 0:n],
                                                  uu[n:P, 4 * x + j, n:P], start=True, stop=True)
                            continue
                        mm = nc.tensor.matmul(m.ps[0:n, 4 + x % 2, j * P:j * P + n], mk[0:n, x % 2, j, 0:n],
                                              rhs(j), start=True, stop=True)
                    mm.then_inc(p_mm, 1)

                def tmul(x, k, n):
                    for j in range(k):
                        mm = nc.tensor.transpose(m.ps[0:n, 2 + x % 2, j * P:j * P + n], uu[0:n, 4 * x + j, 0:n], ident[0:n, 0:n])
                    mm.then_inc(t_mm, 1)

                def rmul(ip, it, x, k, n):
                    if n >= P // 2:
                        pe.wait_ge(p_moved, 13 * h + ip + 1)
                        pe.wait_ge(t_moved, 13 * h + it + 1)
                    if n == P // 2:
                        pe.nop(nofuse=True)
                    for j in range(k):
                        mm = nc.tensor.matmul(m.ps[0:n, 6 + x % 2, j * P:j * P + n], tt[0:n, x % 2, j, 0:n], pp[0:n, x % 2, j, 0:n],
                                              start=True, stop=True)
                    mm.then_inc(r_mm, 1)

                pe.wait_ge(bt_moved, NT * h + NT)
                pe.wait_ge(qk_done, NT * h + NT)
                pe.wait_ge(diff_done, 3 * h + 3)
                for x in range(2):
                    pmul(x, x, 4, P, lambda j: ident)
                if more:
                    group(0, 2, 4 * h + 4)
                for lev in range(1, LEVELS):
                    for x in range(2):
                        pe.wait_ge(u_done, 16 * h + 2 * (lev - 1) + x + 1)
                        if lev > 1:
                            pe.wait_ge(p_moved, 13 * h + 2 * (lev - 2) + x + 1)
                        n = P if lev < LAST else P // 2
                        pmul(2 * lev + x, x, 4, n, lambda j, x=x: uu[:, 4 * x + j, :])
                        tmul(x, 4, n)
                    for x in range(2):
                        rmul(2 * (lev - 1) + x, 2 * (lev - 1) + x, x, 4, n)
                wait_small((p_moved, 13 * h + 12), (mask_done, 16 * h + 15))
                pmul(14, 2, 1, NS, lambda j: ident[0:NS, 0:NS])
                wait_small((u_done, 16 * h + 15), (mask_done, 16 * h + 16))
                pmul(15, 2, 1, NS, lambda j: uu[0:NS, TT, 0:NS])
                tmul(2, 1, NS)
                wait_small((p_moved, 13 * h + 13), (t_moved, 13 * h + 13))
                rmul(12, 12, 2, 1, NS)
                pe.wait_ge(kp_done, h + 1)
                pe.wait_ge(u_done, 16 * h + 16)
                for x in range(3):
                    k, n = (4, P) if x < 2 else (1, NS)
                    if x == 2:
                        pe.wait_ge(w_moved, 3 * h + 1)
                    for j in range(k):
                        t = 4 * x + j
                        mm = nc.tensor.matmul(m.ps[:, 6 + x % 2, j * P:j * P + n], kp[0:n, t, :], uu[0:n, t, 0:n], start=True, stop=True)
                    mm.then_inc(w_mm, 1)
                pe.wait_ge(w_moved, 3 * h + 3)
                pe.wait_ge(vb_done, h + 1)
                pe.wait_ge(kd_done, h + 1)
                pe.wait_ge(t_moved, 13 * h + 13)
                pe.wait_ge(p_moved, 13 * h + 13)
                for t in range(TT):
                    b = t % 2
                    if t >= 2:
                        pe.wait_ge(o_moved, S + t - 1)
                    mm = nc.tensor.matmul(m.ps[:, 2 + b, 0:P], uu[:, t, :], tok[:, t, 2, :], start=True, stop=(t == 0))
                    if t == 0:
                        mm.then_inc(v_mm, 1)
                    else:
                        pe.wait_ge(s_done, S + t)
                        nc.tensor.matmul(m.ps[:, 2 + b, 0:P], kp[:, t, :], st[:, :], start=False, stop=True).then_inc(v_mm, 1)
                        nc.tensor.matmul(m.ps[:, 4 + b, 0:P], bt[:, t, 2, :], st[:, :], start=True, stop=False)
                    if more and t < 6:
                        group(1 + t // 3, t % 3, 4 * h + 5 + t // 3)
                    pe.wait_ge(v_moved, S + t + 1)
                    nc.tensor.matmul(m.ps[:, 6 + b, 0:P], kd[:, t, :], vn[:, b, :], start=True, stop=True).then_inc(s_mm, 1)
                    nc.tensor.matmul(m.ps[:, 4 + b, 0:P], qk_t[:, t, :], vn[:, b, :], start=(t == 0), stop=True).then_inc(o_mm, 1)
                pe.wait_ge(o_moved, S + TT)
                pe.wait_ge(state_in, 16 * h + 16)
                for b in range(NB):
                    nc.tensor.matmul(m.ps[:, 2, 2 * LS * b:2 * LS * b + 2 * LS], sts[:, b, :], wq[:, b, :, :].rearrange("p k l -> p (k l)"),
                                     start=(b == 0), stop=False, skip_group_check=True)
                nc.tensor.matmul(by_sequence(0), tok[0:NS, TT, 2, :], uu[0:NS, TT, 0:NS].rearrange("p (b l) -> p b l", l=LS),
                                 start=False, stop=True, skip_group_check=True).then_inc(v_mm, 1)
                pe.wait_ge(v_moved, S + TT + 1)
                nc.tensor.transpose(m.ps[0:NS, 3, 0:P], vnt[:, 0, :], ident).then_inc(v_mm, 1)
                pe.wait_ge(v_moved, S + TT + 2)
                nc.tensor.matmul(by_sequence(1), vn[0:NS, 0, :], qk_t[0:NS, TT, 0:NS].rearrange("p (b l) -> p b l", l=LS),
                                 start=False, stop=True, skip_group_check=True).then_inc(o_mm, 1)
                pe.wait_ge(km_done, h + 1)
                pe.wait_ge(s_done, S + TT)
                for g in range(2):
                    for b in range(4):
                        mm = nc.tensor.matmul(m.ps[:, 6 + g, b * P:(b + 1) * P], km[:, 4 * g + b, :], vn[0:NS, 0, :], start=True, stop=True)
                    mm.then_inc(s_mm, 1)
                pe.wait_ge(o_moved, S + TT + 1)
                nc.tensor.transpose(m.ps[0:NS, 5, 0:P], vnt[:, 1, :], ident).then_inc(o_mm, 1)
                if more:
                    group(3, 0, 4 * h + 7)
                pe.wait_ge(o_normed, h + 1)
                for g in range(3):
                    for j in range(4 if g < 2 else 1):
                        n = P if g < 2 else NS
                        mm = nc.tensor.transpose(m.ps[:, 2 + g, j * P:j * P + n], orow[0:n, 4 * g + j, :], ident[0:n, 0:n])
                    mm.then_inc(d_mm, 1)

            schedule(pe, first, head)


def split_pair(nc, m, name, src=None, dram=None):
    with ExitStack() as ctx:
        sem = semaphores(nc, ctx, name)
        hi_done, lo_done = sem("hi"), sem("lo")
        BUFS = 4
        full = [sem(f"full{k}") for k in range(BUFS)]
        tmp = ctx.enter_context(nc.sbuf_tensor(name + "tmp", [P, BUFS if src is None else 1, T], F32))
        block = ctx.enter_context(nc.Block())

        def part(f):
            return tmp[:, f % BUFS, :] if src is None else src[:, f, :]

        if src is None:
            @block.sync
            def _(sp):
                for f in range(KT):
                    wait(sp, lo_done, f - BUFS + 1)
                    sp.dma_start(tmp[:, f % BUFS, :], dram[f]).then_inc(full[f % BUFS], 16)

        @block.scalar
        def _(act):
            for f in range(KT):
                if src is None:
                    act.wait_ge(full[f % BUFS], 16 * (f // BUFS + 1))
                nc.scalar.copy(m.p_hi[:, f, :], part(f)).then_inc(hi_done, 1)

        @block.vector
        def _(dve):
            for f in range(KT):
                dve.wait_ge(hi_done, f + 1)
                nc.vector.tensor_tensor(m.p_lo[:, f, :], part(f), m.p_hi[:, f, :].bitcast(F32), ALU.subtract).then_inc(lo_done, 1)


def linear(nc, m, name, w, col0, units, kind, gates=None, beside=None):
    with ExitStack() as ctx:
        sem = semaphores(nc, ctx, name)
        raw_full = [sem("raw_full0"), sem("raw_full1")]
        gate_io = [sem("gate_io0"), sem("gate_io1")]
        hi_done, lo_done, prod, taken, scaled = (sem(n) for n in ("w_hi", "w_lo", "prod", "taken", "scaled"))
        moved = sem("moved")
        gb = ctx.enter_context(nc.sbuf_tensor(name + "gb", [P, 2, T], F32))
        block = ctx.enter_context(nc.Block())
        win = w.rearrange("o (f p) n -> p (o f) n", p=P)
        gated = kind in ("gate", "gate_add")

        def schedule(eng, unit):
            unit(0, 0, True, False)
            unit(1, 1, True, False)
            with eng.Fori(1, units // 2 - 1) as i:
                unit(2 * i, 0, False, False)
                unit(2 * i + 1, 1, False, False)
            unit(units - 2, 0, False, True)
            unit(units - 1, 1, False, True)

        @block.sync
        def _(sp):
            def unit(n, k, first, last):
                if not first:
                    sp.wait_ge(lo_done, n - 1)
                elif k == 1 and beside is not None:
                    sp.dma_start(*beside).then_inc(moved, 16)
                sp.dma_start(m.w_raw[:, k, :].rearrange("p (f n) -> p f n", n=P), win[:, :, bass.ds(col0 + n * P, P)]).then_inc(raw_full[k], 16)
                if gated:
                    if not first:
                        sp.wait_ge(taken, 3 * n - 3)
                    sp.dma_start(gb[:, k, :], gates[bass.ds(n, 1)].rearrange("o p t -> (o p) t")).then_inc(gate_io[k], 16)

            schedule(sp, unit)
            if beside is not None:
                sp.wait_ge(moved, 16)

        @block.scalar
        def _(act):
            def high(n, k):
                act.wait_ge(raw_full[k], 8 * (n - k) + 16)
                nc.scalar.copy(m.w_hi[:, k, :], m.w_raw[:, k, :]).then_inc(hi_done, 1)

            def unit(n, k, first, last):
                if kind == "sigmoid":
                    for c in range(3):
                        act.wait_ge(prod, 3 * n + c + 1)
                        if not first and c == 0:
                            act.wait_ge(gate_io[k], 8 * (n - k))
                        nc.scalar.activation(gb[:, k, cols(c)], m.ps[:, 3 * k + c, 0:CH], ACT.Sigmoid).then_inc(taken, 1)
                else:
                    act.wait_ge(prod, 3 * n + 3)
                if not last:
                    high(n + 2, k)

            high(0, 0)
            high(1, 1)
            schedule(act, unit)

        @block.vector
        def _(dve):
            def low(n, k):
                dve.wait_ge(hi_done, n + 1)
                nc.vector.tensor_tensor(m.w_lo[:, k, :], m.w_raw[:, k, :], m.w_hi[:, k, :].bitcast(F32), ALU.subtract).then_inc(lo_done, 1)

            def unit(n, k, first, last):
                if kind != "sigmoid":
                    for c in range(3):
                        bank = m.ps[:, 3 * k + c, 0:CH]
                        dst = m.acc[:, bass.ds(n, 1), cols(c)].rearrange("p o t -> p (o t)")
                        dve.wait_ge(prod, 3 * n + c + 1)
                        if kind == "copy":
                            nc.vector.tensor_scalar(dst, bank, 1.0, None, ALU.mult).then_inc(taken, 1)
                            continue
                        dve.wait_ge(gate_io[k], 8 * (n - k) + 16)
                        if kind == "gate":
                            nc.vector.tensor_tensor(dst, bank, gb[:, k, cols(c)], ALU.mult).then_inc(taken, 1)
                        else:
                            nc.vector.tensor_tensor(gb[:, k, cols(c)], bank, gb[:, k, cols(c)], ALU.mult).then_inc(scaled, 1)
                            dve.wait_ge(scaled, 3 * n + c + 1)
                            nc.vector.tensor_tensor(dst, dst, gb[:, k, cols(c)], ALU.add).then_inc(taken, 1)
                if not last:
                    low(n + 2, k)

            low(0, 0)
            low(1, 1)
            schedule(dve, unit)

        if kind == "sigmoid":
            @block.gpsimd
            def _(pool):
                with pool.Fori(0, units // 2) as i:
                    for k in range(2):
                        pool.wait_ge(taken, 6 * i + 3 * k + 3)
                        pool.dma_start(gates[bass.ds(2 * i + k, 1)].rearrange("o p t -> (o p) t"), gb[:, k, :]).then_inc(gate_io[k], 16)
                for k in range(2):
                    pool.wait_ge(gate_io[k], 8 * units)

        @block.tensor
        def _(pe):
            def unit(n, k, first, last):
                pe.wait_ge(lo_done, n + 1)
                for c in range(3):
                    if not first:
                        pe.wait_ge(taken, 3 * n + c - 5)
                    for f in range(KT):
                        for j, (a, x) in enumerate(((m.w_hi, m.p_hi), (m.w_hi, m.p_lo), (m.w_lo, m.p_hi))):
                            mm = nc.tensor.matmul(m.ps[:, 3 * k + c, 0:CH], a[:, k, f * P:(f + 1) * P], x[:, f, cols(c)],
                                                  start=(f == 0 and j == 0), stop=(f == KT - 1 and j == 2))
                    mm.then_inc(prod, 1)

            schedule(pe, unit)


class Memory:
    pass


def program(nc, io):
    with ExitStack() as ctx:
        def sb(name, shape, dt=F32, to=ctx):
            return to.enter_context(nc.sbuf_tensor(name, shape, dt))

        m = Memory()
        m.d_const, m.d_rope = io["c_const"], io["c_rope"]
        d_resid = nc.dram_tensor("d_resid", (P, KT, T), F32, kind="Internal").ap()
        d_gates = nc.dram_tensor("d_gates", (2 * KT, P, T), F32, kind="Internal").ap()
        d_oa = nc.dram_tensor("d_oa", (H, P, T), F32, kind="Internal").ap()
        d_ob = nc.dram_tensor("d_ob", (H, P, T), F32, kind="Internal").ap()
        m.cst = sb("cst", [P, NCONST])
        m.gain = sb("gain", [P, 6 * KT + 2])
        m.cst8 = sb("conv_state", [P, CONV_CH // P, NB * (CW - 1)])
        m.convw = sb("conv_weight", [P, CONV_CH // P, CW])
        m.alog = sb("alog", [H, 4])
        m.lam = sb("lam", [P, 2])
        m.comb = sb("comb", [P, 16])
        m.scratch = sb("scratch", [P, 2])
        m.p_hi = sb("p_hi", [P, KT, T], F32R)
        m.p_lo = sb("p_lo", [P, KT, T], F32R)
        m.w_raw = sb("w_raw", [P, 2, D])
        m.w_hi = sb("w_hi", [P, 2, D], F32R)
        m.w_lo = sb("w_lo", [P, 2, D], F32R)
        m.ps = ctx.enter_context(nc.psum_tensor("ps", [P, 8, 512], F32))
        with ExitStack() as step:
            m.resid = sb("resid1", [P, KT, T], to=step)
            load_tokens(nc, m, io["x_prompt"], io["x_sample"])
            small_params(nc, m, [io[n] for n in ("ffn1_pre_norm", "ffn1_post_norm", "mix_pre_norm", "mix_post_norm",
                                                 "ffn2_pre_norm", "ffn2_post_norm")],
                         io["attn_subln"], io["delta_norm"], [io[n] for n in ("lambda_q1", "lambda_k1", "lambda_q2", "lambda_k2")],
                         io["a_log"], io["dt_bias"], io["state_conv"], io["conv_w"])
            m.acc = sb("acc1", [P, KT, T], to=step)
            with ExitStack():
                norms(nc, m, "n1_", pre=0)
                ffn(nc, m, "f1", io["ffn1_w_in"], io["ffn1_w_out"])
                norms(nc, m, "n2_", post=(m.acc, KT, 2.0), pre=2 * KT)
            linear(nc, m, "g1", io["w_in"], OFF_GATE, 2 * KT, "sigmoid", gates=d_gates, beside=(d_resid, m.resid[:, :, :]))
        with ExitStack() as step:
            m.q_s = sb("q_s", [P, H, NS], to=step)
            m.k_s = sb("k_s", [P, H, NS], to=step)
            m.v_s = sb("v_s", [NS, H, P], to=step)
            attention_heads(nc, m, io["w_in"], d_oa, io["k_prompt"], io["v_prompt"], io["k_sample"], io["v_sample"])
            attention_sample(nc, m, io["cache_k"], io["cache_v"], io["page_table"], d_oa)
        with ExitStack() as step:
            m.cols = sb("cols", [P, H, NCOL, NT], to=step)
            delta_gates(nc, m, io["w_in"])
            delta_heads(nc, m, io["w_in"], d_ob, io["state_delta"], io["conv_prompt"], io["conv_sample"],
                        io["delta_prompt"], io["delta_sample"])
        m.resid = sb("resid2", [P, KT, T])
        m.acc = sb("acc2", [P, KT, T])
        split_pair(nc, m, "oa_", dram=d_oa)
        linear(nc, m, "wa_", io["w_a_out"], 0, KT, "gate", gates=d_gates[0:KT],
               beside=(m.resid[:, :, :], d_resid))
        split_pair(nc, m, "ob_", dram=d_ob)
        linear(nc, m, "wb_", io["w_b_out"], 0, KT, "gate_add", gates=d_gates[KT:2 * KT])
        split_pair(nc, m, "mx_", src=m.acc)
        linear(nc, m, "wo_", io["w_o"], 0, KT, "copy")
        norms(nc, m, "n4_", post=(m.acc, 3 * KT, 1.0), pre=4 * KT)
        ffn(nc, m, "f2", io["ffn2_w_in"], io["ffn2_w_out"])
        norms(nc, m, "n6_", post=(m.acc, 5 * KT, 2.0))
        store_tokens(nc, m, io["y_prompt"], io["y_sample"])


_INS = ["x_prompt", "x_sample", "cache_k", "cache_v", "state_conv", "state_delta", "page_table",
        "ffn1_pre_norm", "ffn1_w_in", "ffn1_w_out", "ffn1_post_norm", "mix_pre_norm", "w_in", "conv_w",
        "lambda_q1", "lambda_k1", "lambda_q2", "lambda_k2", "attn_subln", "a_log", "dt_bias", "delta_norm",
        "w_a_out", "w_b_out", "w_o", "mix_post_norm", "ffn2_pre_norm", "ffn2_w_in", "ffn2_w_out", "ffn2_post_norm"]
_OUTS = [("y_prompt", (1, LP, D)), ("y_sample", (NB, LS, D)),
         ("k_prompt", (1, 1, LP, H, P)), ("v_prompt", (1, 1, LP, H, P)),
         ("conv_prompt", (1, 1, CW - 1, CONV_CH)), ("delta_prompt", (1, 1, H, P, P)),
         ("k_sample", (1, NB, LS, H, P)), ("v_sample", (1, NB, LS, H, P)),
         ("conv_sample", (1, NB, CW - 1, CONV_CH)), ("delta_sample", (1, NB, H, P, P))]


def kernel(**inputs):
    import concourse.bacc as _bacc
    from concourse.bass_utils import run_bass_kernel_spmd as _run

    nc = _bacc.Bacc("TRN2", target_bir_lowering=False, num_devices=1)
    arrays, io = {}, {}
    named = {n: np.ascontiguousarray(inputs[n]) for n in _INS}
    named["c_const"], named["c_rope"] = shape_constants()
    for name, a in named.items():
        arrays[f"in_{name}_dram"] = a
        io[name] = nc.dram_tensor(f"in_{name}_dram", a.shape, mybir.dt.from_np(a.dtype), kind="ExternalInput").ap()
    for name, shape in _OUTS:
        io[name] = nc.dram_tensor(f"out_{name}_dram", shape, F32, kind="ExternalOutput").ap()
    program(nc, io)
    r = _run(nc, [arrays], core_ids=[0])
    return tuple(r.results[0][f"out_{name}_dram"] for name, _ in _OUTS)
```
